# Optimizing a Trainium2 kernel written in Bass

```python
import math
import jax, jax.numpy as jnp
from jax import lax
import numpy as np

D_MODEL = 1024
BATCH = 1
SEQ = 512
DEPTH = 2
DEC_BATCH = 8
DEC_SEQ = 1
PAST_LEN = 512
PAGE_SIZE = 128

D_MIX = D_MODEL
ATTN_WIDTH = D_MIX // 2
CONV_CH = D_MIX - ATTN_WIDTH
HEAD_DIM = 64
N_HEADS = ATTN_WIDTH // (2 * HEAD_DIM)
N_SUB = 2 * N_HEADS
V_DIM = 2 * HEAD_DIM
ROT_DIM = HEAD_DIM // 4
ROPE_THETA = 500000.0
CONV_W = 31
CONV_BUF = CONV_W - 1
N_GROUPS = 4
EXP_PER_GROUP = 4
N_EXPERTS = N_GROUPS * EXP_PER_GROUP
TOP_K = 2
D_EXPERT = D_MODEL // 2
Q_BLOCK = 128
EPS = 1e-6
D_IN = 3 * ATTN_WIDTH + 2 * CONV_CH

kernel_name = 'hymba_diffattn_conformer_hiermoe_step'

def rmsnorm(x, g):
    xf = x.astype(jnp.float32)
    y = xf * lax.rsqrt(jnp.mean(xf * xf, axis=-1, keepdims=True) + EPS)
    return (y * g.astype(jnp.float32)).astype(x.dtype)

def layernorm(x, g, b):
    xf = x.astype(jnp.float32)
    mu = jnp.mean(xf, axis=-1, keepdims=True)
    xc = xf - mu
    y = xc * lax.rsqrt(jnp.mean(xc * xc, axis=-1, keepdims=True) + EPS)
    return (y * g.astype(jnp.float32) + b.astype(jnp.float32)).astype(x.dtype)

def rope_partial(x, pos):
    inv = jnp.power(ROPE_THETA, -jnp.arange(0, ROT_DIM, 2, dtype=jnp.float32) / ROT_DIM)
    ang = pos.astype(jnp.float32)[:, None] * inv[None, :]
    cos = jnp.cos(ang)[None, :, None, :]
    sin = jnp.sin(ang)[None, :, None, :]
    xr = x[..., :ROT_DIM].astype(jnp.float32)
    x1, x2 = xr[..., :ROT_DIM // 2], xr[..., ROT_DIM // 2:]
    rot = jnp.concatenate([x1 * cos - x2 * sin, x2 * cos + x1 * sin], axis=-1)
    return jnp.concatenate([rot.astype(x.dtype), x[..., ROT_DIM:]], axis=-1)

def project(h, w_in, q_g, k_g, pos):
    B, T, _ = h.shape
    z = h @ w_in
    q, k, v, a, gt = jnp.split(z, [ATTN_WIDTH, 2 * ATTN_WIDTH, 3 * ATTN_WIDTH, 3 * ATTN_WIDTH + CONV_CH], axis=-1)
    q = rope_partial(rmsnorm(q.reshape(B, T, N_SUB, HEAD_DIM), q_g), pos)
    k = rope_partial(rmsnorm(k.reshape(B, T, N_SUB, HEAD_DIM), k_g), pos)
    v = v.reshape(B, T, N_HEADS, V_DIM)
    u = a * jax.nn.sigmoid(gt)
    return q, k, v, u

def diff_lambda(lq1, lk1, lq2, lk2, lam_init):
    f = jnp.float32
    return (jnp.exp(jnp.sum(lq1.astype(f) * lk1.astype(f))) -
            jnp.exp(jnp.sum(lq2.astype(f) * lk2.astype(f))) + lam_init)

def diff_attend(q, k, v, q_pos, k_pos, lam):
    s = jnp.einsum('bqhd,bkhd->bhqk', q, k, preferred_element_type=jnp.float32) * (HEAD_DIM ** -0.5)
    s = jnp.where(k_pos[None, :] <= q_pos[:, None], s, -jnp.inf)
    p = jax.nn.softmax(s, axis=-1)
    B, _, Tq, Tk = p.shape
    p = p.reshape(B, N_HEADS, 2, Tq, Tk)
    a = (p[:, :, 0] - lam * p[:, :, 1]).astype(v.dtype)
    return jnp.einsum('bhqk,bkhe->bqhe', a, v)

def prompt_attention(q, k, v, lam):
    B, S = q.shape[0], q.shape[1]
    nb = S // Q_BLOCK
    qb = q.reshape(B, nb, Q_BLOCK, N_SUB, HEAD_DIM).transpose(1, 0, 2, 3, 4)
    k_pos = jnp.arange(S, dtype=jnp.int32)

    def blk(args):
        qi, i = args
        q_pos = i * Q_BLOCK + jnp.arange(Q_BLOCK, dtype=jnp.int32)
        return diff_attend(qi, k, v, q_pos, k_pos, lam)

    o = lax.map(blk, (qb, jnp.arange(nb, dtype=jnp.int32)))
    return o.transpose(1, 0, 2, 3, 4).reshape(B, S, N_HEADS, V_DIM)

def diff_finish(o, sub_g, lam_init):
    B, T = o.shape[0], o.shape[1]
    return (rmsnorm(o, sub_g) * (1.0 - lam_init)).reshape(B, T, ATTN_WIDTH)

def conv_branch(u_ext, w, b, ln_g, ln_b):
    y = lax.conv_general_dilated(u_ext, w[:, None, :], window_strides=(1,), padding='VALID',
                                 dimension_numbers=('NWC', 'WIO', 'NWC'),
                                 feature_group_count=CONV_CH) + b
    return jax.nn.silu(layernorm(y, ln_g, ln_b))

def hier_moe(h, w_rg, w_re, w_gate, w_up, w_down):
    B, T, D = h.shape
    x = h.reshape(B * T, D)
    gp = jax.nn.softmax((x @ w_rg).astype(jnp.float32), axis=-1)
    g_idx = jnp.argmax(gp, axis=-1)
    g_w = jnp.max(gp, axis=-1)
    el = (x @ w_re).astype(jnp.float32).reshape(-1, N_GROUPS, EXP_PER_GROUP)
    el = jnp.take_along_axis(el, g_idx[:, None, None], axis=1)[:, 0]
    tv, ti = lax.top_k(el, TOP_K)
    tw = jax.nn.softmax(tv, axis=-1) * g_w[:, None]
    eidx = g_idx[:, None] * EXP_PER_GROUP + ti
    gates = jnp.sum(jax.nn.one_hot(eidx, N_EXPERTS, dtype=jnp.float32) * tw[..., None], axis=1)
    hg = jnp.einsum('nd,edf->nef', x, w_gate)
    hu = jnp.einsum('nd,edf->nef', x, w_up)
    act = jax.nn.silu(hg) * hu * gates[..., None].astype(x.dtype)
    y = jnp.einsum('nef,efd->nd', act, w_down)
    return y.reshape(B, T, D)

def setup_inputs(seed: int = 0) -> dict:
    key = jax.random.key(seed)
    ks = jax.random.split(key, 32)
    f = jnp.float32
    n_pages = PAST_LEN // PAGE_SIZE
    n_phys = (DEC_BATCH * n_pages * 5) // 4
    nrm = lambda k, shape, s: jax.random.normal(k, shape, f) * s
    perm = jax.random.permutation(ks[5], n_phys)[:DEC_BATCH * n_pages]
    return {
        'x_prompt': nrm(ks[0], (BATCH, SEQ, D_MODEL), 1.0),
        'x_sample': nrm(ks[1], (DEC_BATCH, DEC_SEQ, D_MODEL), 1.0),
        'cache_k': nrm(ks[2], (DEPTH, n_phys, PAGE_SIZE, N_SUB, HEAD_DIM), 1.0),
        'cache_v': nrm(ks[3], (DEPTH, n_phys, PAGE_SIZE, N_HEADS, V_DIM), 1.0),
        'state_conv': nrm(ks[4], (DEPTH, DEC_BATCH, CONV_BUF, CONV_CH), 0.5),
        'page_table': perm.reshape(DEC_BATCH, n_pages).astype(jnp.int32),
        'norm1_g': 1.0 + nrm(ks[6], (DEPTH, D_MODEL), 0.02),
        'w_in': nrm(ks[7], (DEPTH, D_MODEL, D_IN), D_MODEL ** -0.5),
        'q_norm_g': 1.0 + nrm(ks[8], (DEPTH, HEAD_DIM), 0.02),
        'k_norm_g': 1.0 + nrm(ks[9], (DEPTH, HEAD_DIM), 0.02),
        'lam_q1': nrm(ks[10], (DEPTH, HEAD_DIM), 0.1),
        'lam_k1': nrm(ks[11], (DEPTH, HEAD_DIM), 0.1),
        'lam_q2': nrm(ks[12], (DEPTH, HEAD_DIM), 0.1),
        'lam_k2': nrm(ks[13], (DEPTH, HEAD_DIM), 0.1),
        'subln_g': 1.0 + nrm(ks[14], (DEPTH, V_DIM), 0.02),
        'conv_w': nrm(ks[15], (DEPTH, CONV_W, CONV_CH), CONV_W ** -0.5),
        'conv_b': nrm(ks[16], (DEPTH, CONV_CH), 0.02),
        'conv_ln_g': 1.0 + nrm(ks[17], (DEPTH, CONV_CH), 0.02),
        'conv_ln_b': nrm(ks[18], (DEPTH, CONV_CH), 0.02),
        'w_out': nrm(ks[19], (DEPTH, D_MIX, D_MODEL), D_MIX ** -0.5),
        'norm2_g': 1.0 + nrm(ks[20], (DEPTH, D_MODEL), 0.02),
        'w_router_group': nrm(ks[21], (DEPTH, D_MODEL, N_GROUPS), D_MODEL ** -0.5),
        'w_router_expert': nrm(ks[22], (DEPTH, D_MODEL, N_EXPERTS), D_MODEL ** -0.5),
        'w_gate': nrm(ks[23], (DEPTH, N_EXPERTS, D_MODEL, D_EXPERT), D_MODEL ** -0.5),
        'w_up': nrm(ks[24], (DEPTH, N_EXPERTS, D_MODEL, D_EXPERT), D_MODEL ** -0.5),
        'w_down': nrm(ks[25], (DEPTH, N_EXPERTS, D_EXPERT, D_MODEL), D_EXPERT ** -0.5),
    }

def reference(x_prompt, x_sample, cache_k, cache_v, state_conv, page_table,
              norm1_g, w_in, q_norm_g, k_norm_g, lam_q1, lam_k1, lam_q2, lam_k2, subln_g,
              conv_w, conv_b, conv_ln_g, conv_ln_b, w_out, norm2_g,
              w_router_group, w_router_expert, w_gate, w_up, w_down):
    B, S, D = x_prompt.shape
    DB, T = x_sample.shape[0], x_sample.shape[1]
    past = page_table.shape[1] * cache_k.shape[2]
    pos_p = jnp.arange(S, dtype=jnp.int32)
    pos_s = past + jnp.arange(T, dtype=jnp.int32)
    kpos_s = jnp.arange(past + T, dtype=jnp.int32)
    xp, xs = x_prompt, x_sample
    kp_l, vp_l, cp_l, ks_l, vs_l, cs_l = [], [], [], [], [], []
    for l in range(DEPTH):
        lam_init = 0.8 - 0.6 * math.exp(-0.3 * l)
        lam = diff_lambda(lam_q1[l], lam_k1[l], lam_q2[l], lam_k2[l], lam_init)

        h = rmsnorm(xp, norm1_g[l])
        q, k, v, u = project(h, w_in[l], q_norm_g[l], k_norm_g[l], pos_p)
        att = diff_finish(prompt_attention(q, k, v, lam), subln_g[l], lam_init)
        u_ext = jnp.pad(u, ((0, 0), (CONV_BUF, 0), (0, 0)))
        cnv = conv_branch(u_ext, conv_w[l], conv_b[l], conv_ln_g[l], conv_ln_b[l])
        xp = xp + jnp.concatenate([att, cnv], axis=-1) @ w_out[l]
        xp = xp + hier_moe(rmsnorm(xp, norm2_g[l]), w_router_group[l], w_router_expert[l],
                           w_gate[l], w_up[l], w_down[l])
        kp_l.append(k); vp_l.append(v); cp_l.append(u_ext[:, -CONV_BUF:])

        h = rmsnorm(xs, norm1_g[l])
        q, k, v, u = project(h, w_in[l], q_norm_g[l], k_norm_g[l], pos_s)
        k_past = cache_k[l, page_table].reshape(DB, past, N_SUB, HEAD_DIM)
        v_past = cache_v[l, page_table].reshape(DB, past, N_HEADS, V_DIM)
        k_all = jnp.concatenate([k_past, k], axis=1)
        v_all = jnp.concatenate([v_past, v], axis=1)
        att = diff_finish(diff_attend(q, k_all, v_all, pos_s, kpos_s, lam), subln_g[l], lam_init)
        u_ext = jnp.concatenate([state_conv[l], u], axis=1)
        cnv = conv_branch(u_ext, conv_w[l], conv_b[l], conv_ln_g[l], conv_ln_b[l])
        xs = xs + jnp.concatenate([att, cnv], axis=-1) @ w_out[l]
        xs = xs + hier_moe(rmsnorm(xs, norm2_g[l]), w_router_group[l], w_router_expert[l],
                           w_gate[l], w_up[l], w_down[l])
        ks_l.append(k); vs_l.append(v); cs_l.append(u_ext[:, -CONV_BUF:])

    return (xp, xs, jnp.stack(kp_l), jnp.stack(vp_l), jnp.stack(cp_l),
            jnp.stack(ks_l), jnp.stack(vs_l), jnp.stack(cs_l))


_drawn_inputs = setup_inputs


def setup_inputs(seed=0):
    import zlib

    import numpy as np

    out = dict(_drawn_inputs(seed))
    spreads = {}
    factors = {'subln_g': 15.433,
     'conv_ln_g': 7.567,
     'conv_ln_b': 16.23,
     'q_norm_g': 4.775,
     'lam_q1': 2.728,
     'lam_k1': 3.981,
     'norm2_g': 7.205}
    for name, (base, spread) in spreads.items():
        noise = np.random.default_rng([zlib.crc32(name.encode()), seed]).standard_normal(out[name].shape)
        drawn = base * np.exp(spread * noise) if base else spread * noise
        out[name] = __import__('jax').numpy.asarray(drawn.astype(out[name].dtype))
    for name, factor in factors.items():
        out[name] = (out[name] * factor).astype(out[name].dtype)
    return out
```

```python
import math
from contextlib import ExitStack

import numpy as np

import concourse.bass as bass
from concourse import mybir

ALU = mybir.AluOpType
ACT = mybir.ActivationFunctionType
AX = mybir.AxisListType.X
F32 = mybir.dt.float32
BF16 = mybir.dt.bfloat16
I32 = mybir.dt.int32
U32 = mybir.dt.uint32

P = 128
D = 1024
KC = D // P
SEQ, DEC = 512, 8
TOK = SEQ + DEC
TILES = SEQ // P + 1
SAMPLE = TILES - 1
DEPTH = 2
HEADS, SUBS, HD, VD = 4, 8, 64, 128
AW = 512
PAGES = 4
N_PHYS = 40
PAST = PAGES * P
TAPS = 31
BUF = TAPS - 1
TAPS_STEP = 15
CH = 4
GROUPS, EPG, EXPERTS = 4, 4, 16
F = 512
FC = F // P
EPS = 1e-6
SCALE = HD ** -0.5
ROT = 8
THETA = 500000.0
RSQRT_SEED = 0x5F3759DF
SLOTS = 6
SLOT_LOADS = 1 + EXPERTS // 2
MAX_SPILL = 8
SPILL_J = 4
PAY = 6
N_PARAM_DMAS = 12
BIG = 3.0e38


def const_layout():
    at, out = 0, {}
    for name, width in (("ident", P), ("before", P), ("ones", P), ("causal", P), ("iota", P),
                        ("cos", TILES * ROT), ("sin", TILES * ROT), ("own_seq", DEC * SUBS),
                        ("row_seq", DEC), ("pair", DEC * HEADS), ("even", 1), ("odd", 1), ("in_seq", 4),
                        ("pad_row", 1), ("valid", TILES), ("expert_of", EXPERTS * SPILL_J),
                        ("spill_j", EXPERTS * SPILL_J), ("spill_no", MAX_SPILL),
                        ("tile_pay", TILES * 3), ("eps", 1)):
        out[name] = (at, width)
        at += width
    return out, at


def const_table():
    where, width = const_layout()
    c = np.zeros((P, width), np.float32)

    def put(name, value):
        a, w = where[name]
        value = np.asarray(value, np.float32)
        c[:value.shape[0], a:a + w] = value.reshape(value.shape[0], w)

    p = np.arange(P)
    put("ident", np.eye(P))
    put("before", p[:, None] < p[None, :])
    put("ones", np.ones((P, P)))
    put("causal", np.where(p[None, :] <= p[:, None], 0.0, -1e30))
    put("iota", np.tile(p, (P, 1)))
    inv = np.power(np.float32(THETA), -np.arange(0, 2 * ROT, 2, dtype=np.float32) / np.float32(2 * ROT))
    pos = np.zeros((P, TILES), np.float32)
    for t in range(SAMPLE):
        pos[:, t] = t * P + p
    pos[:, SAMPLE] = PAST
    angle = (pos[:, :, None] * inv.astype(np.float32)[None, None, :]).astype(np.float32)
    put("cos", np.cos(angle))
    put("sin", np.sin(angle))
    b, h = np.arange(DEC), np.arange(SUBS)
    own = np.zeros((DEC, DEC, SUBS))
    own[b, b, :] = 1
    put("own_seq", own)
    put("row_seq", own.transpose(1, 2, 0).reshape(DEC * SUBS, DEC))
    pair = np.zeros((DEC, SUBS, DEC, HEADS))
    for i in b:
        for j in h:
            pair[i, j, i, j // 2] = 1
    put("pair", pair.reshape(DEC * SUBS, DEC * HEADS))
    put("even", np.tile([1, 0], DEC * HEADS)[:, None])
    put("odd", np.tile([0, 1], DEC * HEADS)[:, None])
    put("in_seq", np.kron(np.eye(4), np.ones((BUF, 1))))
    put("pad_row", TOK + p[:, None])
    valid = np.ones((P, TILES))
    valid[DEC:, SAMPLE] = 0
    put("valid", valid)
    put("expert_of", np.tile(np.repeat(np.arange(EXPERTS), SPILL_J), (P, 1)))
    put("spill_j", np.tile(P * np.tile(np.arange(1, SPILL_J + 1), EXPERTS), (P, 1)))
    put("spill_no", np.tile(np.arange(1, MAX_SPILL + 1), (P, 1)))
    pay = np.zeros((P, TILES, 3))
    pay[:, :, 0] = p[:, None]
    pay[:, :, 1] = np.arange(TILES)[None, :]
    pay[:, :, 2] = 1
    put("tile_pay", pay)
    put("eps", np.full((P, 1), EPS))
    return c


def hybrid_step(nc, a, o, x_rows, xn_rows):
    where, const_width = const_layout()
    w_in = a["w_in"].rearrange("l (c p) n -> l p c n", p=P)
    w_out = a["w_out"].rearrange("l (c p) n -> l p c n", p=P)
    w_gate = a["w_gate"].rearrange("l e (c p) n -> (l e) p c n", p=P)
    w_up = a["w_up"].rearrange("l e (c p) n -> (l e) p c n", p=P)
    w_down = a["w_down"].rearrange("l e (c p) n -> (l e) p c n", p=P)
    cache_k = a["cache_k"].rearrange("l n p h d -> (l n) p (h d)")
    cache_v = a["cache_v"].rearrange("l n p h d -> (l n) p (h d)")
    k_prompt = o["k_prompt"].rearrange("l b (t p) h d -> l (b t) p (h d)", p=P)
    v_prompt = o["v_prompt"].rearrange("l b (t p) h d -> l (b t) p (h d)", p=P)
    k_sample = o["k_sample"].rearrange("l b t h d -> l (b t) (h d)")
    v_sample = o["v_sample"].rearrange("l b t h d -> l (b t) (h d)")

    with ExitStack() as ctx:
        def sb(name, shape, dt=F32):
            return ctx.enter_context(nc.sbuf_tensor(name, shape, dt))

        def sem(name):
            return ctx.enter_context(nc.semaphore(name))

        x = sb("x", [P, TILES, D])
        feat = sb("feat", [P, KC, TOK])
        ring = sb("ring", [P, SLOTS, KC * AW])
        w_last = sb("w_last", [P, KC * AW])
        v_rows = sb("v_rows", [P, TILES, AW])
        qk_t = sb("qk_t", [P, 2, HEADS, AW])
        u_t = sb("u_t", [P, CH, BUF + SEQ])
        conv = sb("conv", [P, CH, TOK])
        probs = sb("probs", [P, 4, AW])
        const = sb("const", [P, const_width])

        def cs(name, rows=P):
            at, width = where[name]
            return const[0:rows, at:at + width]

        ident = cs("ident")
        ones = cs("ones")
        pages = x[:, 0:4, :].rearrange("p t n -> p (t n)").rearrange("p (s n) -> p s n", n=AW)
        half4 = x[:, 4, :].rearrange("p (s n) -> p s n", n=AW)
        sig_rows = half4
        q_rep = half4
        att_t = half4
        qk_prod = w_last[:, :].rearrange("p (s g n) -> p s g n", s=2, g=PAGES)
        qk_rows = probs[:, 0:2, :]
        qk_sq = probs[:, 2:4, :]
        state = probs[0:4 * BUF, 0:2, :]
        state_w = probs[0:4 * BUF, 2, :]
        conv_w_rows = probs[0:TAPS, 3, :]
        u_last = qk_t[0:BUF, 0, 0, :]
        u_new = qk_t[0:DEC, 0, 1, :]
        qk_new = qk_t[0:DEC, 0, 2, :]
        o_rows = u_t[:, 0, BUF:]
        o_sq = u_t[:, 1, BUF:]
        probs_flat = probs[:, :, :].rearrange("p s n -> p (s n)")
        s_dec = u_t[0:DEC * SUBS, 3, 0:PAST + 1]
        rs_conv = probs_flat[:, 0:TOK]
        qk_flat = qk_t[:, :, :, :].rearrange("p a h n -> p (a h n)")
        xe = qk_flat[:, 0:2 * D].rearrange("p (s n) -> p s n", s=2)
        ye = qk_flat[:, 2 * D:4 * D].rearrange("p (s n) -> p s n", s=2)
        xe_t = probs_flat.rearrange("p (s c n) -> p s c n", s=2, n=P)
        v_flat = v_rows[:, :, :].rearrange("p t n -> p (t n)")
        hid = v_flat[:, 0:2 * F].rearrange("p (s n) -> p s n", s=2)
        hid_t = v_flat[:, 2 * F:4 * F].rearrange("p (s c n) -> p s c n", s=2, n=P)
        spill_a = u_t[:, 0, BUF:].rearrange("p (s n) -> p s n", s=MAX_SPILL)
        spill_b = u_t[:, 1, BUF:].rearrange("p (s n) -> p s n", s=MAX_SPILL)

        conv_flat = conv[:, :, :].rearrange("p c n -> p (c n)")
        vec_rows = qk_flat[0:32, 2048:2048 + P]
        lam_vec = qk_flat[:, 3072:3072 + 4 * HD].rearrange("p (s n) -> p s n", n=HD)
        vec = sb("vec", [P, 32])
        G1, G2, CB, LG, LB, SUB = 0, 8, 16, 20, 24, 28
        head_rows = sb("head_rows", [P, 2, HD])
        lam_rows = sb("lam_rows", [P, 2])
        conv_w = sb("conv_w", [P, CH, TAPS])
        w_route = sb("w_route", [P, KC, GROUPS + EXPERTS])
        u_smp = sb("u_smp", [P, CH, DEC])
        sig_smp = sb("sig_smp", [P, 2, DEC])
        q_smp = v_rows[32:32 + DEC, SAMPLE, :]
        sc_dec = sb("sc_dec", [P, PAGES, DEC * SUBS])
        small = sb("small", [P, 64])
        ss = sb("ss", [P, 16])
        rs = sb("rs", [P, 16])
        tmp = sb("tmp", [P, 32])
        newton = sb("newton", [P, 32])
        rope = qk_sq[:, 0, :].rearrange("p (s n) -> p s n", s=4)
        mx = sb("mx", [P, 2, 4])
        zs = sb("zs", [P, 2, 2])
        rz = sb("rz", [P, 2, HEADS])
        sn = sb("sn", [DEC, SUBS])
        sn_x = sb("sn_x", [DEC, DEC * SUBS])
        c_dec = u_t[0:DEC * SUBS, 2, BUF:BUF + 40]
        wide_flat = feat[:, 4:6, :].rearrange("p s n -> p (s n)")[:, 0:DEC * PAGES * DEC * HEADS]
        a_wide = wide_flat.rearrange("p (b g n) -> p b g n", b=DEC, g=PAGES)
        o_wide = qk_t[0:DEC * HEADS, 0, 0, :]
        a_new = u_t[0:DEC, 2, BUF + 256:BUF + 288]
        o_dec = u_t[:, 2, BUF + 288:BUF + 384].rearrange("p (s n) -> p s n", s=3)
        pick = conv_flat[:, 0:480].rearrange("p (s n) -> p s n", s=6)
        slot_f = conv_flat[:, 1680:1824].rearrange("p (e c) -> p e c", c=3 + PAY)
        logit = conv_flat[:, 528:628].rearrange("p (t n) -> p t n", t=TILES)
        chosen = conv_flat[:, 1840:1840 + (TILES + 1) * EXPERTS]
        few = conv_flat[:, 628:708].rearrange("p (s t) -> p s t", t=TILES)
        key = conv_flat[:, 708:788].rearrange("p (t e) -> p t e", t=TILES)
        pay = conv_flat[:, 788:1028].bitcast(BF16).rearrange("p (t e c) -> p t e c", t=TILES, c=PAY)
        hot = conv_flat[:, 1040:1680].bitcast(BF16).rearrange("p (s t n) -> p s t n", s=2, n=P)
        gate = sb("gate", [P, EXPERTS + 1])
        rows_g = sb("rows_g", [P, EXPERTS + 1], U32)
        sp_f = sb("sp_f", [P, 3 * MAX_SPILL + 4])
        sp_i = sb("sp_i", [1, MAX_SPILL + 4], I32)
        cnt = sb("cnt", [P, EXPERTS])
        pt = sb("pt", [1, DEC * PAGES], I32)

        bank = [ctx.enter_context(nc.psum_tensor(f"bank{i}", [P, 512], F32)) for i in range(8)]

        start_in = sem("start_in")
        clear_ok = sem("clear_ok")
        layer_go = sem("layer_go")
        slot_in = [sem(f"slot_in{s}") for s in range(SLOTS)]
        slot_used = [sem(f"slot_used{s}") for s in range(SLOTS)]
        last_in = sem("last_in")
        x_in = sem("x_in")
        x_again = sem("x_again")
        page_in = [sem(f"page_in{s}") for s in range(8)]
        k_used = sem("k_used")
        v_used = sem("v_used")
        params_in = sem("params_in")
        params_go = sem("params_go")
        vec_ps = sem("vec_ps")
        vec_ok = sem("vec_ok")
        lam_sum = sem("lam_sum")
        lam_exp = sem("lam_exp")
        sq_ok = sem("sq_ok")
        xn_ok = sem("xn_ok")
        turn_ps = sem("turn_ps")
        feat_ok = sem("feat_ok")
        u_ps = sem("u_ps")
        sig_ok = sem("sig_ok")
        u_ok = sem("u_ok")
        st_ok = sem("st_ok")
        st_ps = sem("st_ps")
        ut_ps = sem("ut_ps")
        ut_ok = sem("ut_ok")
        u_out = sem("u_out")
        qkv_ps = sem("qkv_ps")
        v_ok = sem("v_ok")
        v_out = sem("v_out")
        qsq_ok = sem("qsq_ok")
        qsq_read = sem("qsq_read")
        qk_free = sem("qk_free")
        qk_ok = sem("qk_ok")
        k_out = sem("k_out")
        q_smp_ok = sem("q_smp_ok")
        qkt_ps = sem("qkt_ps")
        qkt_ok = sem("qkt_ok")
        rep_ps = sem("rep_ps")
        rep_ok = sem("rep_ok")
        prod_read = sem("prod_read")
        s_ps = sem("s_ps")
        max_ok = sem("max_ok")
        exp_ok = sem("exp_ok")
        a_ok = sem("a_ok")
        at_ps = sem("at_ps")
        at_ok = sem("at_ok")
        pv_ps = sem("pv_ps")
        o_ok = sem("o_ok")
        ot_ps = sem("ot_ps")
        ot_ok = sem("ot_ok")
        dec_in = sem("dec_in")
        dec_s = sem("dec_s")
        dec_m = sem("dec_m")
        dec_e = sem("dec_e")
        dec_c = sem("dec_c")
        dec_a = sem("dec_a")
        dec_ok = sem("dec_ok")
        dec_o = sem("dec_o")
        dec_w = sem("dec_w")
        dec_t = sem("dec_t")
        dec_q = sem("dec_q")
        dec_r = sem("dec_r")
        dec_f = sem("dec_f")
        conv_ok = sem("conv_ok")
        mean_ps = sem("mean_ps")
        xc_ok = sem("xc_ok")
        csq_ok = sem("csq_ok")
        var_ps = sem("var_ps")
        std_ok = sem("std_ok")
        cn_ok = sem("cn_ok")
        cat_ok = sem("cat_ok")
        wo_ps = sem("wo_ps")
        x2_ok = sem("x2_ok")
        sq2_ok = sem("sq2_ok")
        xn2_ok = sem("xn2_ok")
        turn2_ps = sem("turn2_ps")
        feat2_ok = sem("feat2_ok")
        rows_out = sem("rows_out")
        log_ps = sem("log_ps")
        r_d = sem("r_d")
        r_e = sem("r_e")
        m_ok = sem("m_ok")
        cum_ps = sem("cum_ps")
        hot_ok = sem("hot_ok")
        idx_ps = sem("idx_ps")
        idx_ok = sem("idx_ok")
        spill_ok = sem("spill_ok")
        xe_in = [sem("xe_in0"), sem("xe_in1")]
        xt_ps = sem("xt_ps")
        xt_ok = sem("xt_ok")
        gu_ps = sem("gu_ps")
        silu_ok = sem("silu_ok")
        hid_ok = sem("hid_ok")
        ht_ps = sem("ht_ps")
        ht_ok = sem("ht_ok")
        dn_ps = sem("dn_ps")
        y_ok = sem("y_ok")
        y_add = sem("y_add")
        sp_w = sem("sp_w")
        sp_hot = sem("sp_hot")
        sp_idx = sem("sp_idx")
        sp_rows = sem("sp_rows")
        sp_xe = sem("sp_xe")
        sp_xt = sem("sp_xt")
        sp_xtok = sem("sp_xtok")
        sp_gu = sem("sp_gu")
        sp_silu = sem("sp_silu")
        sp_hid = sem("sp_hid")
        sp_ht = sem("sp_ht")
        sp_htok = sem("sp_htok")
        sp_dn = sem("sp_dn")
        sp_y = sem("sp_y")
        sp_add = sem("sp_add")
        tick = sem("tick")
        pe_tick = sem("pe_tick")
        act_tick = sem("act_tick")
        pool_tick = sem("pool_tick")
        final_out = sem("final_out")

        order = [SAMPLE] + list(range(SAMPLE))
        rows_of = [P] * SAMPLE + [DEC]
        items = [(qt, h) for qt in range(SAMPLE) for h in range(HEADS)]

        def cols(t):
            return slice(t * P, t * P + rows_of[t])

        block = ctx.enter_context(nc.Block())

        @block.sync
        def _(sp):
            def unit(weights, s, load, l):
                dst = ring[:, s, :].rearrange("p (c n) -> p c n", n=weights.shape[3])
                sp.wait_ge(slot_used[s], l * SLOT_LOADS + load + 1)
                sp.sem_inc(tick, 1)
                sp.dma_start(dst, weights.rearrange("a p c n -> p (a c) n"))\
                    .then_inc(slot_in[s], 16)

            sp.sem_inc(params_go, 1)
            for s in range(SLOTS):
                sp.sem_inc(slot_used[s], 1)
            sp.dma_start(const[:, :], a["const"]).then_inc(start_in, 16)
            sp.dma_start(pt[:, :], a["page_table"].rearrange("(a b) g -> a (b g)", a=1)).then_inc(start_in, 16)
            sp.dma_start(x_rows[SEQ:TOK, :], a["x_sample"].rearrange("b s d -> (b s) d")).then_inc(start_in, 16)
            sp.wait_ge(start_in, 48)
            sp.wait_ge(y_add, 32)
            sp.sem_inc(layer_go, 1)

            with sp.Fori(0, DEPTH) as l:
                sp.wait_ge(layer_go, l + 1)
                sp.sem_inc(tick, 1)
                sp.dma_start(x[:, 0:4, :], x_rows[0:SEQ, :].rearrange("(t p) n -> p t n", p=P)).then_inc(x_in, 16)
                sp.dma_start(x[0:DEC, 4, :], x_rows[SEQ:TOK, :]).then_inc(x_in, 16)
                sp.wait_ge(params_in, l * 16 * N_PARAM_DMAS + 16 * N_PARAM_DMAS)
                for s, u in enumerate((3, 4, 0, 1, 2)):
                    unit(w_in[bass.ds(l, 1), :, :, u * AW:(u + 1) * AW], s, 0, l)
                unit(w_out[bass.ds(l, 1), :, :, 0:AW], 5, 0, l)

                def page(cache, s, i):
                    n = sp.value_load(pt[0:1, bass.ds(i, 1)], min_val=0, max_val=N_PHYS - 1)
                    sp.dma_start(pages[:, s, :], cache[bass.ds(l * N_PHYS + n, 1)].rearrange("a p n -> p (a n)"))\
                        .then_inc(page_in[s], 16)

                sp.wait_ge(turn_ps, l * 10 + 10)
                sp.sem_inc(tick, 1)
                for j in range(8):
                    page(cache_k, j, j)
                with sp.Fori(1, 4) as g:
                    for half in range(2):
                        sp.wait_ge(k_used, l * 8 + g * 2 + (half - 1))
                        sp.sem_inc(tick, 1)
                        for j in range(4):
                            page(cache_k, half * 4 + j, g * 8 + (half * 4 + j))
                for half in range(2):
                    sp.wait_ge(k_used, l * 8 + 7 + half)
                    sp.sem_inc(tick, 1)
                    for j in range(4):
                        page(cache_v, half * 4 + j, half * 4 + j)
                sp.wait_ge(prod_read, l * 8 + 10)
                sp.sem_inc(tick, 1)
                sp.dma_start(w_last[:, :].rearrange("p (c n) -> p c n", n=AW),
                             w_out[bass.ds(l, 1), :, :, AW:].rearrange("a p c n -> p (a c) n")).then_inc(last_in, 16)
                with sp.Fori(1, 4) as g:
                    for half in range(2):
                        sp.wait_ge(v_used, l * 8 + g * 2 + (half - 1))
                        sp.sem_inc(tick, 1)
                        for j in range(4):
                            page(cache_v, half * 4 + j, g * 8 + (half * 4 + j))
                sp.wait_ge(v_used, l * 8 + 8)
                sp.sem_inc(tick, 1)
                sp.dma_start(x[:, 0:4, :], x_rows[0:SEQ, :].rearrange("(t p) n -> p t n", p=P)).then_inc(x_again, 16)
                sp.wait_ge(pv_ps, l * 16 + 16)
                sp.sem_inc(tick, 1)
                sp.dma_start(x[0:DEC, 4, :], x_rows[SEQ:TOK, :]).then_inc(x_again, 16)
                with sp.Fori(0, EXPERTS // 2) as g:
                    for half in range(2):
                        for j, w in enumerate((w_gate, w_up, w_down)):
                            unit(w[bass.ds(l * EXPERTS + g * 2 + half, 1)], half * 3 + j, g + 1, l)
                sp.wait_ge(spill_ok, l + 1)
                sp.sem_inc(tick, 1)
                n_spill = sp.value_load(sp_i[0:1, 0:1], min_val=0, max_val=MAX_SPILL)
                before = sp.value_load(sp_i[0:1, 1:2], min_val=0, max_val=DEPTH * MAX_SPILL)
                with sp.If(n_spill > 0):
                    sp.wait_ge(dn_ps, l * EXPERTS + EXPERTS)
                    sp.sem_inc(tick, 1)
                    with sp.Fori(0, n_spill) as i:
                        e = sp.value_load(sp_i[0:1, bass.ds(i + 2, 1)], min_val=0, max_val=EXPERTS - 1)
                        for j, w in enumerate((w_gate, w_up, w_down)):
                            sp.dma_start(ring[:, j, :].rearrange("p (c n) -> p c n", n=w.shape[3]),
                                         w[bass.ds(l * EXPERTS + e, 1)].rearrange("a p c n -> p (a c) n"))\
                                .then_inc(sp_w, 16)
                        sp.wait_ge(sp_dn, before + i + 1)
                        sp.sem_inc(tick, 1)
            sp.wait_ge(layer_go, DEPTH + 1)
            sp.dma_start(o["y_prompt"].rearrange("b s d -> (b s) d"), x_rows[0:SEQ, :]).then_inc(final_out, 16)
            sp.dma_start(o["y_sample"].rearrange("b s d -> (b s) d"), x_rows[SEQ:TOK, :]).then_inc(final_out, 16)
            sp.wait_ge(final_out, 32)
            sp.wait_ge(u_out, DEPTH * 48)
            sp.wait_ge(v_out, DEPTH * 80)
            sp.wait_ge(k_out, DEPTH * 80)

        @block.tensor
        def _(pe):
            def turn(dst, src, rows):
                return pe.transpose(dst, src, ident[0:rows, 0:rows])

            pe.wait_ge(start_in, 48)
            with pe.Fori(0, DEPTH) as l:
                pe.wait_ge(params_in, l * 16 * N_PARAM_DMAS + 16 * N_PARAM_DMAS)
                pe.sem_inc(pe_tick, 1)
                turn(bank[0][:, 0:29], vec_rows[0:29, :], 29)
                for c in range(CH):
                    mm = turn(bank[1][:, c * TAPS:(c + 1) * TAPS], conv_w_rows[:, c * P:(c + 1) * P], TAPS)
                mm.then_inc(vec_ps, 1)
                for t in range(TILES):
                    pe.wait_ge(xn_ok, l * TILES + t + 1)
                    for g in range(2):
                        b = 4 + 2 * (t % 2) + g
                        if t >= 2:
                            pe.wait_ge(feat_ok, l * 10 + 2 * (t - 2) + g + 1)
                        if t == SAMPLE:
                            pe.sem_inc(pe_tick, 1)
                        for c in range(4):
                            mm = turn(bank[b][:, c * P:c * P + rows_of[t]],
                                      x[0:rows_of[t], t, (4 * g + c) * P:(4 * g + c + 1) * P], rows_of[t])
                        mm.then_inc(turn_ps, 1)
                pe.wait_ge(feat_ok, l * 10 + 10)
                pe.wait_ge(vec_ok, l + 1)
                for c in range(CH):
                    if c >= 2:
                        pe.wait_ge(u_ok, l * CH + c - 1)
                    for half in range(2):
                        if c == 0:
                            pe.wait_ge(slot_in[half], l * 16 * SLOT_LOADS + 16)
                        main, smp = bank[2 * (c % 2) + half], bank[4 + c % 2][:, half * DEC:(half + 1) * DEC]
                        for k in range(KC):
                            w = ring[:, half, k * AW + c * P:k * AW + (c + 1) * P]
                            pe.matmul(main[:, :], w, feat[:, k, 0:SEQ], start=(k == 0), stop=(k == KC - 1))
                            mm = pe.matmul(smp, w, feat[:, k, SEQ:TOK], start=(k == 0), stop=(k == KC - 1))
                        if c == CH - 1:
                            mm.then_inc(slot_used[half], 1)
                    if c == CH - 1:
                        pe.matmul(bank[6][0:1, 0:1], ones[:, 0:1], ones[:, 0:1], start=True, stop=True)\
                            .then_inc(u_ps, 1)
                    else:
                        mm.then_inc(u_ps, 1)
                pe.wait_ge(st_ok, l + 1)
                for c in range(CH):
                    for j in range(2):
                        mm = pe.matmul(bank[7][:, c * DEC + 4 * j:c * DEC + 4 * j + 4],
                                       state[:, j, c * P:(c + 1) * P], cs("in_seq", 4 * BUF), start=True, stop=True)
                mm.then_inc(st_ps, 1)

                def qkv(i):
                    t = order[i]
                    if i < 2:
                        pe.wait_ge(u_ok, l * CH + 3 + i)
                    if i >= 2:
                        pe.wait_ge(qk_free, l * TILES + i - 1)
                    if i >= 1:
                        pe.wait_ge(v_ok, l * TILES + i)
                    dst = (bank[2 * (i % 2)], bank[2 * (i % 2) + 1], bank[4])
                    for k in range(KC):
                        for j in range(3):
                            if i == 0 and k == 0:
                                pe.wait_ge(slot_in[2 + j], l * 16 * SLOT_LOADS + 16)
                            mm = pe.matmul(dst[j][0:rows_of[t], :], feat[:, k, cols(t)],
                                           ring[:, 2 + j, k * AW:(k + 1) * AW], start=(k == 0), stop=(k == KC - 1))
                            if i == TILES - 1 and k == KC - 1:
                                mm.then_inc(slot_used[2 + j], 1)
                    if i == TILES - 1:
                        pe.wait_ge(rep_ok, l * DEC + 6)
                        mm = pe.matmul(bank[7][0:1, 0:1], ones[:, 0:1], ones[:, 0:1], start=True, stop=True)
                    mm.then_inc(qkv_ps, 1)

                def turn_qk(i):
                    pe.wait_ge(qk_ok, l * TILES + i + 1)
                    if i >= 2:
                        pe.wait_ge(qkt_ok, l * SAMPLE + i - 1)
                    for j in range(2):
                        for h in range(HEADS):
                            mm = turn(bank[5 + j][:, h * P:(h + 1) * P], qk_rows[:, j, h * P:(h + 1) * P], P)
                    mm.then_inc(qkt_ps, 1)

                def spread(b):
                    if b == 0:
                        pe.wait_ge(q_smp_ok, l + 1)
                        pe.wait_ge(conv_ok, l * 2 + 1)
                    else:
                        pe.wait_ge(rep_ok, l * DEC + b)
                    pe.matmul(bank[7][:, :], ident[32:32 + DEC, 32 + b:33 + b].to_broadcast([DEC, P]), q_smp,
                              start=True, stop=True).then_inc(rep_ps, 1)

                def turn_u():
                    pe.wait_ge(u_ok, l * CH + 4)
                    for c in range(CH):
                        turn(bank[5][0:BUF, c * P:(c + 1) * P], u_t[:, c, SEQ:SEQ + BUF], P)
                    for c in range(CH):
                        mm = turn(bank[6][0:DEC, c * P:(c + 1) * P], u_smp[:, c, :], P)
                    mm.then_inc(ut_ps, 1)

                qkv(0)
                qkv(1)
                spread(0)
                turn_u()
                spread(1)
                for i in range(2, TILES):
                    qkv(i)
                    if i == 2:
                        pe.wait_ge(ut_ok, l + 1)
                    spread(2 * i - 2)
                    turn_qk(i - 1)
                    if i < 4:
                        spread(2 * i - 1)
                spread(7)
                turn_qk(TILES - 1)

                def scores(n):
                    qt, h = items[n]
                    if n == 0:
                        pe.wait_ge(qkt_ok, l * SAMPLE + SAMPLE)
                        pe.wait_ge(qk_free, l * TILES + TILES)
                    if n >= 2:
                        pe.wait_ge(exp_ok, l * 16 + n - 1)
                    width = (qt + 1) * P
                    for j in range(2):
                        mm = pe.matmul(bank[2 * (n % 2) + j][:, 0:width], qk_t[64 * j:64 * j + 64, 0, h, cols(qt)],
                                       qk_t[64 * j:64 * j + 64, 1, h, 0:width], start=True, stop=True)
                    mm.then_inc(s_ps, 1)

                def turn_att(n):
                    qt, h = items[n]
                    pe.wait_ge(a_ok, l * 16 + n + 1)
                    if n >= 1:
                        pe.wait_ge(at_ok, l * 16 + n)
                    if n == 0:
                        pe.wait_ge(v_ok, l * TILES + TILES)
                    for c in range(qt + 1):
                        mm = turn(bank[4][:, c * P:(c + 1) * P], probs[:, 2 * (n % 2), c * P:(c + 1) * P], P)
                    mm.then_inc(at_ps, 1)

                def values(n):
                    qt, h = items[n]
                    pe.wait_ge(at_ok, l * 16 + n + 1)
                    if h == 0 and qt >= 1:
                        pe.wait_ge(o_ok, l * 2 * SAMPLE + 2 * qt - 1)
                    for c in range(qt + 1):
                        mm = pe.matmul(bank[6][:, h * P:(h + 1) * P], att_t[:, n % 2, c * P:(c + 1) * P],
                                       v_rows[:, c, h * P:(h + 1) * P], start=(c == 0), stop=(c == qt))
                    mm.then_inc(pv_ps, 1)

                def turn_o(qt):
                    pe.wait_ge(o_ok, l * 2 * SAMPLE + 2 * qt + 2)
                    if qt >= 1:
                        pe.wait_ge(ot_ok, l * SAMPLE + qt)
                    else:
                        pe.wait_ge(dec_m, l + 1)
                    if qt == 2:
                        pe.wait_ge(xc_ok, l * 2 + 2)
                    for h in range(HEADS):
                        mm = turn(bank[7][:, h * P:(h + 1) * P], o_rows[:, h * P:(h + 1) * P], P)
                    mm.then_inc(ot_ps, 1)

                def sampled_scores():
                    pe.wait_ge(dec_in, l + 1)
                    pe.sem_inc(pe_tick, 1)
                    for g in range(PAGES):
                        turn(bank[5][0:DEC * SUBS, g * P:(g + 1) * P], sc_dec[:, g, :], P)
                    pe.matmul(bank[7][0:DEC * SUBS, 0:1], sn_x[:, :], ones[0:DEC, 0:1], start=True, stop=True)\
                        .then_inc(dec_s, 1)

                def sampled_weights():
                    pe.wait_ge(dec_c, l + 1)
                    for g in range(PAGES):
                        pe.matmul(bank[5][:, g * 32:(g + 1) * 32], s_dec[:, g * P:(g + 1) * P], c_dec[:, 0:32],
                                  start=True, stop=True)
                    pe.matmul(bank[5][0:DEC, P:P + 32], c_dec[:, 32:40], c_dec[:, 0:32], start=True, stop=True)\
                        .then_inc(dec_a, 1)

                def sampled_new_values():
                    pe.wait_ge(dec_ok, l + 1)
                    pe.sem_inc(pe_tick, 1)
                    pe.matmul(bank[5][0:DEC * HEADS, :], a_new, v_rows[0:DEC, SAMPLE, :], start=True, stop=False)

                def sampled_values(b):
                    for j in range(PAGES):
                        slot = (b % 2) * PAGES + j
                        pe.wait_ge(page_in[slot], l * 128 + (b // 2) * 16 + 80)
                        mm = pe.matmul(bank[5][0:DEC * HEADS, :], a_wide[:, b, j, :], pages[:, slot, :],
                                       start=False, stop=(b == DEC - 1 and j == PAGES - 1))
                    mm.then_inc(v_used, 1)

                pe.wait_ge(rep_ok, l * DEC + DEC)
                scores(0)
                scores(1)
                for n in range(16):
                    if n + 2 < 16:
                        scores(n + 2)
                    turn_att(n)
                    if n >= 1:
                        values(n - 1)
                    if n % 4 == 2 and n > 4:
                        turn_o(n // 4 - 1)
                    if n == 5:
                        sampled_scores()
                    if n == 7:
                        sampled_weights()
                    if n == 8:
                        sampled_new_values()
                    if n >= 8:
                        sampled_values(n - 8)
                    if n == 11:
                        pe.wait_ge(conv_ok, l * 2 + 2)
                        pe.wait_ge(ot_ok, l * SAMPLE + 2)
                        for c in range(CH):
                            mm = pe.matmul(bank[7][:, :], ones, conv[:, c, 0:SEQ], start=(c == 0), stop=(c == CH - 1))
                        mm.then_inc(mean_ps, 1)
                    if n == 13:
                        pe.wait_ge(xc_ok, l * 2 + 1)
                        for c in range(CH):
                            mm = pe.matmul(bank[7][:, 0:DEC], ones, conv[:, c, SEQ:TOK], start=(c == 0),
                                           stop=(c == CH - 1))
                        mm.then_inc(mean_ps, 1)
                values(15)

                pe.wait_ge(exp_ok, l * 16 + 16)
                pe.matmul(bank[2][0:1, 0:1], ones[:, 0:1], ones[:, 0:1], start=True, stop=True).then_inc(dec_o, 1)

                def variances():
                    pe.wait_ge(csq_ok, l + 1)
                    for c in range(CH):
                        pe.matmul(bank[2][:, :], ones, feat[:, 4 + c, 0:SEQ], start=(c == 0), stop=(c == CH - 1))
                    for c in range(CH):
                        mm = pe.matmul(bank[3][:, 0:DEC], ones, feat[:, 4 + c, SEQ:TOK], start=(c == 0),
                                       stop=(c == CH - 1))
                    mm.then_inc(var_ps, 1)

                def sampled_turn():
                    pe.wait_ge(dec_w, l + 1)
                    pe.sem_inc(pe_tick, 1)
                    for h in range(HEADS):
                        mm = turn(bank[4][:, h * 32:(h + 1) * 32], o_wide[:, h * P:(h + 1) * P], 32)
                    mm.then_inc(dec_t, 1)

                def sampled_norms():
                    pe.wait_ge(dec_q, l + 1)
                    pe.matmul(bank[5][:, 0:32], ones, o_dec[:, 1, :], start=True, stop=True).then_inc(dec_r, 1)

                def project(t, ks):
                    if t == 0 and ks[0] == 0:
                        pe.wait_ge(slot_in[5], l * 16 * SLOT_LOADS + 16)
                        pe.wait_ge(last_in, l * 16 + 16)
                        pe.wait_ge(ot_ok, l * SAMPLE + SAMPLE - 1)
                    if t == 0 and ks[0] == 4:
                        pe.wait_ge(cat_ok, l + 1)
                    if t == 1 and ks[0] == 0:
                        pe.wait_ge(std_ok, l + 1)
                    if t == SAMPLE - 1 and ks[0] == 0:
                        pe.wait_ge(ot_ok, l * SAMPLE + SAMPLE)
                    if t == SAMPLE and ks[0] == 0:
                        pe.wait_ge(dec_f, l + 1)
                    if t >= 2 and ks[0] == 0:
                        pe.wait_ge(x2_ok, l * TILES + t - 1)
                    for k in ks:
                        for j, w in enumerate((ring[:, 5, :], w_last)):
                            mm = pe.matmul(bank[2 * (t % 2) + j][0:rows_of[t], :], feat[:, k, cols(t)],
                                           w[:, k * AW:(k + 1) * AW], start=(k == 0), stop=(k == KC - 1))
                            if t == TILES - 1 and k == KC - 1 and j == 0:
                                mm.then_inc(slot_used[5], 1)
                    if ks[-1] == KC - 1:
                        mm.then_inc(wo_ps, 1)

                def turn_route(t):
                    pe.wait_ge(xn2_ok, l * TILES + t + 1)
                    for g in range(2):
                        if t >= 1:
                            pe.wait_ge(feat2_ok, l * 10 + 2 * (t - 1) + g + 1)
                        if t == SAMPLE:
                            pe.sem_inc(pe_tick, 1)
                        for c in range(4):
                            mm = turn(bank[4 + g][:, c * P:c * P + rows_of[t]],
                                      x[0:rows_of[t], t, (4 * g + c) * P:(4 * g + c + 1) * P], rows_of[t])
                        mm.then_inc(turn2_ps, 1)

                def route(t):
                    pe.wait_ge(feat2_ok, l * 10 + 2 * t + 2)
                    for k in range(KC):
                        mm = pe.matmul(bank[6][0:rows_of[t], t * 20:t * 20 + 20], feat[:, k, cols(t)],
                                       w_route[:, k, :], start=(k == 0), stop=(k == KC - 1))
                    mm.then_inc(log_ps, 1)

                variances()
                project(0, range(0, 4))
                sampled_turn()
                turn_o(SAMPLE - 1)
                sampled_norms()
                project(0, range(4, KC))
                for t in range(1, TILES):
                    project(t, range(0, 6))
                    turn_route(t - 1)
                    project(t, range(6, KC))
                    route(t - 1)
                turn_route(TILES - 1)
                route(TILES - 1)

                pe.wait_ge(m_ok, l + 1)
                width = TILES * EXPERTS
                pe.matmul(bank[7][:, 0:width + EXPERTS], cs("before"), chosen, start=True, stop=True)
                for later in range(1, TILES + 1):
                    mm = pe.matmul(bank[7][:, later * EXPERTS:width + EXPERTS], ones,
                                   chosen[:, 0:(TILES + 1 - later) * EXPERTS], start=False, stop=True,
                                   skip_group_check=True)
                mm.then_inc(cum_ps, 1)
                for e in range(EXPERTS):
                    pe.wait_ge(hot_ok, l * EXPERTS + e + 1)
                    for t in range(TILES):
                        mm = pe.matmul(bank[0][:, e * PAY:(e + 1) * PAY], hot[:, e % 2, t, :], pay[:, t, e, :],
                                       start=(t == 0), stop=(t == TILES - 1))
                    mm.then_inc(idx_ps, 1)

                def gathered(b, n16, turned_before=None):
                    if turned_before is not None:
                        pe.wait_ge(ht_ok, turned_before)
                    pe.wait_ge(xe_in[b], n16)
                    for g in range(2):
                        for c in range(4):
                            mm = turn(bank[6 + g][:, c * P:(c + 1) * P],
                                      xe[:, b, (4 * g + c) * P:(4 * g + c + 1) * P], P)
                        mm.then_inc(xt_ps, 1)

                def gate_up(b, n, ks, slot_count):
                    if ks[0] == 0:
                        pe.wait_ge(xt_ok, n * 2 + 2)
                        pe.wait_ge(slot_in[3 * b], slot_count)
                        pe.wait_ge(slot_in[3 * b + 1], slot_count)
                    for k in ks:
                        for j in range(2):
                            mm = pe.matmul(bank[2 + 2 * b + j][:, :], xe_t[:, b, k, :],
                                           ring[:, 3 * b + j, k * F:(k + 1) * F], start=(k == 0), stop=(k == KC - 1))
                            if k == KC - 1:
                                mm.then_inc(slot_used[3 * b + j], 1)
                    if ks[-1] == KC - 1:
                        pe.matmul(bank[7][0:1, 0:1], ones[:, 0:1], ones[:, 0:1], start=True, stop=True)\
                            .then_inc(gu_ps, 1)

                def turn_hidden(b, n):
                    pe.wait_ge(hid_ok, n + 1)
                    for c in range(FC):
                        mm = turn(bank[6][:, c * P:(c + 1) * P], hid[:, b, c * P:(c + 1) * P], P)
                    mm.then_inc(ht_ps, 1)

                def down(b, n, slot_count):
                    pe.wait_ge(ht_ok, n + 1)
                    pe.wait_ge(slot_in[3 * b + 2], slot_count)
                    pe.wait_ge(y_ok, n * 2 + 1)
                    for k in range(FC):
                        for j in range(2):
                            mm = pe.matmul(bank[j][:, :], hid_t[:, b, k, :],
                                           ring[:, 3 * b + 2, k * D + j * F:k * D + (j + 1) * F],
                                           start=(k == 0), stop=(k == FC - 1))
                    mm.then_inc(slot_used[3 * b + 2], 1)
                    pe.matmul(bank[2 + 2 * b][0:1, 0:1], ones[:, 0:1], ones[:, 0:1], start=True, stop=True)\
                        .then_inc(dn_ps, 1)

                pe.wait_ge(idx_ok, l + 1)
                gathered(0, l * 128 + 16)
                gate_up(0, pe.snap(l * EXPERTS), range(KC), l * 16 * SLOT_LOADS + 32)
                gathered(1, l * 128 + 16)
                with pe.Fori(0, EXPERTS // 2 - 1) as g:
                    n = pe.snap(l * EXPERTS + g * 2)
                    loads = pe.snap(l * 16 * SLOT_LOADS + g * 16 + 32)
                    gate_up(1, n + 1, range(4), loads)
                    turn_hidden(0, n)
                    gate_up(1, n + 1, range(4, KC), loads)
                    gathered(0, l * 128 + g * 16 + 32, n + 1)
                    down(0, n, loads)
                    gate_up(0, n + 2, range(4), loads + 16)
                    turn_hidden(1, n + 1)
                    gate_up(0, n + 2, range(4, KC), loads + 16)
                    gathered(1, l * 128 + g * 16 + 32, n + 2)
                    down(1, n + 1, loads)
                n = pe.snap(l * EXPERTS + EXPERTS - 2)
                loads = pe.snap(l * 16 * SLOT_LOADS + 16 * SLOT_LOADS)
                gate_up(1, n + 1, range(4), loads)
                turn_hidden(0, n)
                gate_up(1, n + 1, range(4, KC), loads)
                down(0, n, loads)
                turn_hidden(1, n + 1)
                down(1, n + 1, loads)

                pe.wait_ge(spill_ok, l + 1)
                pe.sem_inc(pe_tick, 1)
                n_spill = pe.value_load(sp_i[0:1, 0:1], min_val=0, max_val=MAX_SPILL)
                before = pe.value_load(sp_i[0:1, 1:2], min_val=0, max_val=DEPTH * MAX_SPILL)
                with pe.If(n_spill > 0):
                    pe.wait_ge(y_ok, l * 32 + 33)
                    pe.sem_inc(pe_tick, 1)
                    with pe.Fori(0, n_spill) as i:
                        m = pe.snap(before + i)
                        e = pe.value_load(sp_i[0:1, bass.ds(i + 2, 1)], min_val=0, max_val=EXPERTS - 1)
                        pe.wait_ge(sp_hot, m + 1)
                        for t in range(TILES):
                            mm = pe.matmul(bank[0][:, 0:PAY], hot[:, 0, t, :],
                                           pay[:, t, bass.ds(e, 1), :].rearrange("p a c -> p (a c)"),
                                           start=(t == 0), stop=(t == TILES - 1))
                        mm.then_inc(sp_idx, 1)
                        pe.wait_ge(sp_xe, m * 16 + 16)
                        for g in range(2):
                            for c in range(4):
                                mm = turn(bank[6 + g][:, c * P:(c + 1) * P],
                                          xe[:, 0, (4 * g + c) * P:(4 * g + c + 1) * P], P)
                        mm.then_inc(sp_xt, 1)
                        pe.wait_ge(sp_xtok, m + 1)
                        pe.wait_ge(sp_w, m * 48 + 48)
                        for k in range(KC):
                            for j in range(2):
                                mm = pe.matmul(bank[2 + j][:, :], xe_t[:, 0, k, :], ring[:, j, k * F:(k + 1) * F],
                                               start=(k == 0), stop=(k == KC - 1))
                        mm.then_inc(sp_gu, 1)
                        pe.wait_ge(sp_hid, m + 1)
                        for c in range(FC):
                            mm = turn(bank[6][:, c * P:(c + 1) * P], hid[:, 0, c * P:(c + 1) * P], P)
                        mm.then_inc(sp_ht, 1)
                        pe.wait_ge(sp_htok, m + 1)
                        for k in range(FC):
                            for j in range(2):
                                mm = pe.matmul(bank[j][:, :], hid_t[:, 0, k, :],
                                               ring[:, 2, k * D + j * F:k * D + (j + 1) * F],
                                               start=(k == 0), stop=(k == FC - 1))
                        mm.then_inc(sp_dn, 1)
                pe.wait_ge(layer_go, l + 2)

        @block.scalar
        def _(act):
            act.sem_inc(y_ok, 1)
            with act.Fori(0, DEPTH) as l:
                act.wait_ge(params_go, l + 1)
                at_l = bass.ds(l, 1)
                act.dma_start(vec_rows[0:29, :], a["vectors"][at_l].rearrange("a c p -> (a c) p"))\
                    .then_inc(params_in, 16)
                act.dma_start(head_rows[:, :, :].rearrange("p s n -> p (s n)"),
                              a["heads"][at_l, 0:2 * HD].to_broadcast([P, 2 * HD])).then_inc(params_in, 16)
                act.dma_start(lam_vec.rearrange("p s n -> p (s n)"),
                              a["heads"][at_l, 2 * HD:].to_broadcast([P, 4 * HD])).then_inc(params_in, 16)
                act.dma_start(lam_rows[:, :], a["lam_init"][at_l].to_broadcast([P, 2])).then_inc(params_in, 16)
                act.dma_start(conv_w_rows, a["conv_w"][at_l].rearrange("a w c -> (a w) c")).then_inc(params_in, 16)
                act.dma_start(w_route[:, :, :], a["w_router"][at_l]
                              .rearrange("a (c p) n -> p (a c) n", p=P)).then_inc(params_in, 16)
                for j in range(2):
                    act.dma_start(state[:, j, :], a["state_conv"][at_l]
                                  .rearrange("a b w c -> (a b w) c")[4 * BUF * j:4 * BUF * (j + 1), :])\
                        .then_inc(params_in, 16)
                for j in range(4):
                    act.dma_start(state_w[j * BUF:(j + 1) * BUF, :],
                                  a["conv_w"][at_l].rearrange("a w c -> (a w) c")[0:BUF, :]).then_inc(params_in, 16)
                act.wait_ge(start_in, 48)
                act.wait_ge(clear_ok, 1)
                act.wait_ge(x_in, l * 32 + 32)
                for t in (0, 1, SAMPLE):
                    n = rows_of[t]
                    junk = feat[0:n, 2 * (t % 2):2 * (t % 2) + 2, 0:AW]
                    last = act.activation(junk, x[0:n, t, :].rearrange("p (s n) -> p s n", s=2), ACT.Square,
                                          accum_out=ss[0:n, t:t + 1])
                    act.drain()
                act.drain().then_inc(sq_ok, 1)
                act.wait_ge(lam_sum, l + 1)
                act.activation(small[:, 2:4], small[:, 0:2], ACT.Exp).then_inc(lam_exp, 1)
                for c in range(CH):
                    act.wait_ge(u_ps, l * CH + c + 1)
                    if c >= 2:
                        act.wait_ge(u_ok, l * CH + c - 1)
                    act.activation(sig_rows[:, c % 2, :], bank[2 * (c % 2) + 1][:, :], ACT.Sigmoid)
                    act.activation(sig_smp[:, c % 2, :], bank[4 + c % 2][:, DEC:2 * DEC], ACT.Sigmoid)\
                        .then_inc(sig_ok, 1)
                def rows_of_u():
                    act.wait_ge(ut_ps, l + 1)
                    act.activation(u_last, bank[5][0:BUF, :], ACT.Copy)
                    act.activation(u_new, bank[6][0:DEC, :], ACT.Copy).then_inc(ut_ok, 1)
                    act.wait_ge(ut_ok, l + 1)
                    act.dma_start(o["conv_prompt"][at_l].rearrange("a b w c -> (a b w) c"), u_last).then_inc(u_out, 16)
                    act.dma_start(o["conv_sample"][at_l].rearrange("a b w c -> (a b) w c")[:, BUF - 1, :], u_new)\
                        .then_inc(u_out, 16)
                    act.dma_start(o["conv_sample"][at_l].rearrange("a b w c -> (a b) w c")[:, 0:BUF - 1, :],
                                  a["state_conv"][at_l].rearrange("a b w c -> (a b) w c")[:, 1:BUF, :])\
                        .then_inc(u_out, 16)

                def squares(i):
                    t = order[i]
                    n = rows_of[t]
                    act.wait_ge(qkv_ps, l * TILES + i + 1)
                    if i >= 1:
                        act.wait_ge(qsq_read, l * TILES + i)
                    else:
                        act.wait_ge(st_ps, l + 1)
                    for j in range(2):
                        last = act.activation(qk_sq[0:n, j, :], bank[2 * (i % 2) + j][0:n, :], ACT.Square)
                    last.then_inc(qsq_ok, 1)
                    act.activation(v_rows[0:n, t, :], bank[4][0:n, :], ACT.Copy).then_inc(v_ok, 1)
                    act.wait_ge(v_ok, l * TILES + i + 1)
                    dst = v_sample[at_l] if t == SAMPLE else v_prompt[at_l][:, t]
                    act.dma_start(dst.rearrange("a p n -> (a p) n"), v_rows[0:n, t, :]).then_inc(v_out, 16)

                def keys_out(i):
                    t = order[i]
                    n = rows_of[t]
                    act.wait_ge(qk_ok, l * TILES + i + 1)
                    dst = k_sample[at_l] if t == SAMPLE else k_prompt[at_l][:, t]
                    act.dma_start(dst.rearrange("a p n -> (a p) n"), qk_rows[0:n, 1, :]).then_inc(k_out, 16)
                    if i >= 1:
                        act.wait_ge(qkt_ps, l * SAMPLE + i)
                        if i == 1:
                            act.wait_ge(u_out, l * 48 + 48)
                        for j in range(2):
                            last = act.activation(qk_t[:, j, :, cols(t)],
                                                  bank[5 + j][:, :].rearrange("p (h n) -> p h n", h=HEADS), ACT.Copy)
                        last.then_inc(qkt_ok, 1)

                def replicate(b):
                    act.wait_ge(rep_ps, l * DEC + b + 1)
                    if b >= 2:
                        act.wait_ge(k_used, l * DEC + b - 1)
                    act.activation(q_rep[:, b % 2, :], bank[7][:, :], ACT.Copy).then_inc(rep_ok, 1)

                squares(0)
                keys_out(0)
                squares(1)
                replicate(0)
                rows_of_u()
                replicate(1)
                for i in range(2, TILES):
                    squares(i)
                    replicate(2 * i - 2)
                    keys_out(i - 1)
                    if i < 4:
                        replicate(2 * i - 1)
                replicate(7)
                keys_out(TILES - 1)

                def exps(n):
                    qt, h = items[n]
                    width = (qt + 1) * P
                    act.wait_ge(max_ok, l * 16 + n + 1)
                    if n == 0:
                        act.wait_ge(k_out, l * 80 + 80)
                    if n >= 2:
                        act.wait_ge(at_ps, l * 16 + n - 1)
                    for j in range(2):
                        last = act.activation(probs[:, 2 * (n % 2) + j, 0:width], bank[2 * (n % 2) + j][:, 0:width],
                                              ACT.Exp, bias=mx[:, n % 2, j:j + 1], scale=SCALE,
                                              accum_out=zs[:, n % 2, j:j + 1])
                    last.then_inc(exp_ok, 1)

                def weights_out(n):
                    qt, h = items[n]
                    width = (qt + 1) * P
                    act.wait_ge(at_ps, l * 16 + n + 1)
                    if n == 0:
                        act.wait_ge(k_used, l * DEC + DEC)
                    if n >= 2:
                        act.wait_ge(pv_ps, l * 16 + n - 1)
                    act.activation(att_t[:, n % 2, 0:width], bank[4][:, 0:width], ACT.Copy).then_inc(at_ok, 1)

                def heads_out(qt):
                    act.wait_ge(ot_ps, l * SAMPLE + qt + 1)
                    act.activation(feat[:, 0:HEADS, cols(qt)], bank[7][:, :].rearrange("p (h n) -> p h n", h=HEADS),
                                   ACT.Copy, scale=vec[:, SUB + 1:SUB + 2]).then_inc(ot_ok, 1)

                exps(0)
                exps(1)
                for n in range(16):
                    weights_out(n)
                    if n + 2 < 16:
                        exps(n + 2)
                    if n == 6:
                        act.wait_ge(dec_m, l + 1)
                        act.activation(s_dec, s_dec, ACT.Exp, bias=small[0:DEC * SUBS, 9:10], scale=SCALE,
                                       accum_out=small[0:DEC * SUBS, 10:11]).then_inc(dec_e, 1)
                    if n % 4 == 2 and n > 4:
                        heads_out(n // 4 - 1)

                act.wait_ge(dec_o, l + 1)
                act.wait_ge(xc_ok, l * 2 + 2)
                for c in range(CH):
                    last = act.activation(feat[:, 4 + c, :], conv[:, c, :], ACT.Square)
                last.then_inc(csq_ok, 1)
                act.activation(o_wide, bank[5][0:DEC * HEADS, :], ACT.Copy).then_inc(dec_w, 1)
                act.wait_ge(var_ps, l + 1)
                act.activation(rs_conv[:, 0:SEQ], bank[2][:, :], ACT.Sqrt, bias=cs("eps"), scale=1.0 / AW)
                act.activation(rs_conv[:, SEQ:TOK], bank[3][:, 0:DEC], ACT.Sqrt, bias=cs("eps"), scale=1.0 / AW)\
                    .then_inc(std_ok, 1)
                heads_out(SAMPLE - 1)
                act.wait_ge(cn_ok, l + 1)
                for c in range(CH):
                    last = act.activation(feat[:, 4 + c, :], conv[:, c, :], ACT.Silu, bias=vec[:, LB + c:LB + c + 1],
                                          scale=vec[:, LG + c:LG + c + 1])
                last.then_inc(cat_ok, 1)

                for t in range(TILES):
                    n = rows_of[t]
                    if t >= 1:
                        act.drain()
                    act.wait_ge(x2_ok, l * TILES + t + 1)
                    act.activation(qk_t[0:n, 0, 0:2, :], x[0:n, t, :].rearrange("p (s n) -> p s n", s=2), ACT.Square,
                                   accum_out=ss[0:n, t:t + 1]).then_inc(sq2_ok, 1)
                    act.dma_start(x_rows[t * P:t * P + n, :], x[0:n, t, :]).then_inc(rows_out, 16)
                    act.wait_ge(xn2_ok, l * TILES + t + 1)
                    act.dma_start(xn_rows[t * P:t * P + n, :], x[0:n, t, :]).then_inc(rows_out, 16)

                act.wait_ge(r_d, l * 2 + 1)
                act.activation(pick[:, 2, 0:TILES * GROUPS], pick[:, 1, 0:TILES * GROUPS], ACT.Exp).then_inc(r_e, 1)
                act.wait_ge(r_d, l * 2 + 2)
                act.activation(few[:, 7, :], few[:, 6, :], ACT.Exp).then_inc(r_e, 1)

                def silu(b, n):
                    act.wait_ge(gu_ps, n + 1)
                    act.activation(hid[:, b, :], bank[2 + 2 * b][:, :], ACT.Silu).then_inc(silu_ok, 1)

                def hidden_out(b, n):
                    act.wait_ge(ht_ps, n + 1)
                    act.activation(hid_t[:, b, :, :], bank[6][:, :].rearrange("p (c n) -> p c n", c=FC), ACT.Copy)\
                        .then_inc(ht_ok, 1)

                def y_half(b, n, e):
                    act.wait_ge(dn_ps, n + 1)
                    act.wait_ge(y_add, n * 16 + 16)
                    act.activation(ye[:, b, 0:F], bank[0][:, :], ACT.Copy, scale=gate[:, bass.ds(e, 1)])\
                        .then_inc(y_ok, 1)

                n0 = act.snap(l * EXPERTS)
                act.wait_ge(idx_ok, l + 1)
                silu(0, n0)
                with act.Fori(0, EXPERTS // 2 - 1) as g:
                    n = act.snap(l * EXPERTS + g * 2)
                    hidden_out(0, n)
                    silu(1, n + 1)
                    y_half(0, n, g * 2)
                    hidden_out(1, n + 1)
                    silu(0, n + 2)
                    y_half(1, n + 1, g * 2 + 1)
                n = act.snap(l * EXPERTS + EXPERTS - 2)
                hidden_out(0, n)
                silu(1, n + 1)
                y_half(0, n, EXPERTS - 2)
                hidden_out(1, n + 1)
                y_half(1, n + 1, EXPERTS - 1)

                act.wait_ge(spill_ok, l + 1)
                act.sem_inc(act_tick, 1)
                n_spill = act.value_load(sp_i[0:1, 0:1], min_val=0, max_val=MAX_SPILL)
                before = act.value_load(sp_i[0:1, 1:2], min_val=0, max_val=DEPTH * MAX_SPILL)
                with act.If(n_spill > 0):
                    with act.Fori(0, n_spill) as i:
                        m = act.snap(before + i)
                        act.wait_ge(sp_gu, m + 1)
                        act.activation(hid[:, 0, :], bank[2][:, :], ACT.Silu).then_inc(sp_silu, 1)
                        act.wait_ge(sp_ht, m + 1)
                        act.activation(hid_t[:, 0, :, :], bank[6][:, :].rearrange("p (c n) -> p c n", c=FC), ACT.Copy)\
                            .then_inc(sp_htok, 1)
                        act.wait_ge(sp_dn, m + 1)
                        act.activation(ye[:, 0, 0:F], bank[0][:, :], ACT.Copy, scale=gate[:, EXPERTS:EXPERTS + 1])\
                            .then_inc(sp_y, 1)

        @block.gpsimd
        def _(pool):
            pool.dma_start(x_rows[0:SEQ, :], a["x_prompt"].rearrange("b s d -> (b s) d")).then_inc(y_add, 16)
            pool.dma_start(x_rows[TOK:TOK + P, :], a["x_prompt"].rearrange("b s d -> (b s) d")[0:P, :])\
                .then_inc(y_add, 16)
            pool.wait_ge(start_in, 48)
            with pool.Fori(0, DEPTH) as l:
                with pool.Fori(0, 4) as g:
                    for half in range(2):
                        for j in range(4):
                            pool.wait_ge(page_in[half * 4 + j], l * 128 + g * 16 + 16)
                        pool.wait_ge(rep_ok, l * DEC + g * 2 + (half + 1))
                        pool.wait_ge(prod_read, l * DEC + g * 2 + (half + 1))
                        pool.tensor_tensor(
                            qk_prod[:, half, :, :], pages[:, half * 4:half * 4 + 4, :],
                            q_rep[:, half:half + 1, :].to_broadcast([P, PAGES, AW]), ALU.mult)\
                            .then_inc(k_used, 1)
                pool.wait_ge(rows_out, l * 160 + 160)
                pool.wait_ge(idx_ok, l + 1)
                pool.sem_inc(pool_tick, 1)

                def gather(e):
                    b = e % 2
                    if e >= 2:
                        pool.wait_ge(xt_ps, l * 32 + 2 * (e - 2) + 2)
                        pool.sem_inc(pool_tick, 1)
                    pool.indirect_dma_start(out=xe[:, b, :], out_offset=None, in_=xn_rows[:, :],
                                            in_offset=bass.IndirectOffsetOnAxis(ap=rows_g[:, e:e + 1], axis=0),
                                            bounds_check=TOK - 1, oob_is_err=False).then_inc(xe_in[b], 16)

                def add_rows(e):
                    b = e % 2
                    pool.wait_ge(y_ok, l * 32 + 2 * e + 3)
                    pool.wait_ge(y_add, l * 256 + 16 * e + 32)
                    pool.sem_inc(pool_tick, 1)
                    pool.indirect_dma_start(out=x_rows[:, :],
                                            out_offset=bass.IndirectOffsetOnAxis(ap=rows_g[:, e:e + 1], axis=0),
                                            in_=ye[:, b, :], in_offset=None, compute_op=ALU.add)\
                        .then_inc(y_add, 16)

                gather(0)
                gather(1)
                gather(2)
                for e in range(EXPERTS):
                    if e + 3 < EXPERTS:
                        gather(e + 3)
                    add_rows(e)
                pool.wait_ge(y_add, l * 256 + 288)
                pool.wait_ge(spill_ok, l + 1)
                pool.sem_inc(pool_tick, 1)
                n_spill = pool.value_load(sp_i[0:1, 0:1], min_val=0, max_val=MAX_SPILL)
                before = pool.value_load(sp_i[0:1, 1:2], min_val=0, max_val=DEPTH * MAX_SPILL)
                with pool.If(n_spill > 0):
                    with pool.Fori(0, n_spill) as i:
                        m = pool.snap(before + i)
                        pool.wait_ge(sp_rows, m + 1)
                        pool.sem_inc(pool_tick, 1)
                        pool.indirect_dma_start(
                            out=xe[:, 0, :], out_offset=None, in_=xn_rows[:, :],
                            in_offset=bass.IndirectOffsetOnAxis(ap=rows_g[:, EXPERTS:EXPERTS + 1], axis=0),
                            bounds_check=TOK - 1, oob_is_err=False).then_inc(sp_xe, 16)
                        pool.wait_ge(sp_y, m * 2 + 2)
                        pool.sem_inc(pool_tick, 1)
                        pool.indirect_dma_start(
                            out=x_rows[:, :],
                            out_offset=bass.IndirectOffsetOnAxis(ap=rows_g[:, EXPERTS:EXPERTS + 1], axis=0),
                            in_=ye[:, 0, :], in_offset=None, compute_op=ALU.add).then_inc(sp_add, 16)
                        pool.wait_ge(sp_add, m * 16 + 16)
                pool.sem_inc(params_go, 1)
                pool.sem_inc(layer_go, 1)

        @block.vector
        def _(v):
            def tt(out, in0, in1, op):
                return v.tensor_tensor(out, in0, in1, op)

            def rsqrt(out, ssum, n, scale, rows=P):
                m, r, t = tmp[0:rows, 0:n], out, newton[0:rows, 0:n]
                v.tensor_scalar(m, ssum, scale, EPS, ALU.mult, ALU.add)
                v.drain()
                v.tensor_scalar(t.bitcast(I32), m.bitcast(I32), 1, None, ALU.logical_shift_right)
                v.drain()
                v.tensor_scalar(r.bitcast(I32), t.bitcast(I32), -1.0, float(RSQRT_SEED), ALU.mult, ALU.add)
                v.drain()
                for _ in range(3):
                    v.scalar_tensor_tensor(t, r, -0.5, r, ALU.mult, ALU.mult)
                    v.drain()
                    tt(t, t, m, ALU.mult)
                    v.drain()
                    v.scalar_tensor_tensor(r, t, 1.5, r, ALU.add, ALU.mult)
                    v.drain()

            v.wait_ge(start_in, 48)
            v.sem_inc(prod_read, 2)
            v.memset(u_t[:, :, 0:BUF], 0.0)
            v.memset(ss[:, :], 1.0)
            v.memset(sp_f[:, :], 0.0)
            v.drain().then_inc(clear_ok, 1)
            with v.Fori(0, DEPTH) as l:
                v.wait_ge(x_in, l * 32 + 32)
                for t in (2, 3):
                    v.tensor_tensor_reduce(out=feat[:, 2 * t:2 * t + 2, 0:AW],
                                           in0=x[:, t, :].rearrange("p (s n) -> p s n", s=2),
                                           in1=x[:, t, :].rearrange("p (s n) -> p s n", s=2), scale=1.0, scalar=0.0,
                                           op0=ALU.mult, op1=ALU.add, accum_out=ss[:, t:t + 1])
                v.drain()
                v.wait_ge(sq_ok, l + 1)
                rsqrt(rs[:, 0:TILES], ss[:, 0:TILES], TILES, 1.0 / D)
                for t in range(TILES):
                    n = rows_of[t]
                    v.tensor_scalar(x[0:n, t, :], x[0:n, t, :], rs[0:n, t:t + 1], None, ALU.mult).then_inc(xn_ok, 1)
                v.wait_ge(vec_ps, l + 1)
                v.tensor_copy(vec[:, 0:29], bank[0][:, 0:29])
                v.tensor_copy(conv_w[:, :, :], bank[1][:, 0:CH * TAPS].rearrange("p (c w) -> p c w", c=CH))\
                    .then_inc(vec_ok, 1)
                v.tensor_tensor_reduce(out=qk_prod[:, 0, 0, 0:HD], in0=lam_vec[:, 0, :], in1=lam_vec[:, 1, :],
                                       scale=1.0, scalar=0.0, op0=ALU.mult, op1=ALU.add, accum_out=small[:, 0:1])
                v.tensor_tensor_reduce(out=qk_prod[:, 0, 1, 0:HD], in0=lam_vec[:, 2, :], in1=lam_vec[:, 3, :],
                                       scale=1.0, scalar=0.0, op0=ALU.mult, op1=ALU.add, accum_out=small[:, 1:2])
                v.drain().then_inc(lam_sum, 1)
                tt(vec[:, SUB + 1:SUB + 2], vec[:, SUB:SUB + 1], lam_rows[:, 1:2], ALU.mult)
                for t in range(TILES):
                    n = rows_of[t]
                    for g in range(2):
                        v.wait_ge(turn_ps, l * 10 + 2 * t + g + 1)
                        b = bank[4 + 2 * (t % 2) + g][:, :].rearrange("p (c n) -> p c n", c=4)[:, :, 0:n]
                        tt(feat[:, 4 * g:4 * g + 4, cols(t)], b,
                           vec[:, G1 + 4 * g:G1 + 4 * g + 4].unsqueeze(2).to_broadcast([P, 4, n]), ALU.mult)\
                            .then_inc(feat_ok, 1)
                v.wait_ge(lam_exp, l + 1)
                tt(small[:, 4:5], small[:, 3:4], small[:, 2:3], ALU.subtract)
                v.drain()
                tt(small[:, 4:5], small[:, 4:5], lam_rows[:, 0:1], ALU.subtract)
                def glu(c):
                    v.wait_ge(sig_ok, l * CH + c + 1)
                    tt(u_t[:, c, BUF:], bank[2 * (c % 2)][:, :], sig_rows[:, c % 2, :], ALU.mult)
                    tt(u_smp[:, c, :], bank[4 + c % 2][:, 0:DEC], sig_smp[:, c % 2, :], ALU.mult).then_inc(u_ok, 1)

                def convolve(c, first=0, last=(TAPS - 1) // TAPS_STEP):
                    acc = conv[:, c, 0:SEQ]
                    v.drain()
                    if first == 0:
                        v.tensor_scalar(acc, u_t[:, c, 0:SEQ], conv_w[:, c, 0:1], vec[:, CB + c:CB + c + 1],
                                        ALU.mult, ALU.add)
                        v.drain()
                    with v.Fori(first, last) as g:
                        for i in range(TAPS_STEP):
                            w = g * TAPS_STEP + (i + 1)
                            v.scalar_tensor_tensor(acc, u_t[:, c, bass.ds(w, SEQ)], conv_w[:, c, bass.ds(w, 1)], acc,
                                                   ALU.mult, ALU.add)
                            v.drain()

                def rows_norm(i):
                    t = order[i]
                    n = rows_of[t]
                    v.wait_ge(qsq_ok, l * TILES + i + 1)
                    v.tensor_reduce(ss[0:n, 0:16], qk_sq[0:n, :, :].rearrange("p s (h d) -> p (s h) d", d=HD), AX,
                                    ALU.add)
                    v.drain()
                    rsqrt(rs[0:n, 0:16], ss[0:n, 0:16], 16, 1.0 / HD, n)
                    if i == 1:
                        v.drain()
                    if i >= 1:
                        v.wait_ge(k_out, l * 80 + 16 * i)
                    if i >= 2:
                        v.wait_ge(qkt_ps, l * SAMPLE + i - 1)
                    for j in range(2):
                        last = tt(qk_rows[0:n, j, :].rearrange("p (h d) -> p h d", d=HD),
                                  bank[2 * (i % 2) + j][0:n, :].rearrange("p (h d) -> p h d", d=HD),
                                  rs[0:n, 8 * j:8 * j + 8].unsqueeze(2).to_broadcast([n, SUBS, HD]), ALU.mult)
                    last.then_inc(qk_free, 1)
                    v.drain()
                    for j in range(2):
                        q4 = qk_rows[0:n, j, :].rearrange("p (h d) -> p h d", d=HD)
                        tt(q4, q4, head_rows[0:n, j:j + 1, :].to_broadcast([n, SUBS, HD]), ALU.mult)
                    v.drain()
                    both = qk_rows[0:n, :, :].rearrange("p s (h d) -> p (s h) d", d=HD)
                    x1, x2 = both[:, :, 0:ROT], both[:, :, ROT:2 * ROT]
                    tab = [cs(name)[0:n, t * ROT:(t + 1) * ROT].unsqueeze(1).to_broadcast([n, 16, ROT])
                           for name in ("cos", "sin")]
                    r = [rope[0:n, j, :].rearrange("p (h d) -> p h d", d=ROT) for j in range(4)]
                    tt(r[0], x1, tab[0], ALU.mult)
                    tt(r[1], x2, tab[1], ALU.mult)
                    tt(r[2], x2, tab[0], ALU.mult)
                    tt(r[3], x1, tab[1], ALU.mult)
                    v.drain()
                    tt(x1, r[0], r[1], ALU.subtract)
                    tt(x2, r[2], r[3], ALU.add)
                    v.drain().then_inc(qk_ok, 1)
                    v.engine_nop().then_inc(qsq_read, 1)

                def score_sums(b):
                    v.wait_ge(k_used, l * DEC + b + 1)
                    for g in range(PAGES):
                        last = v.tensor_reduce(sc_dec[:, g, b * SUBS:(b + 1) * SUBS],
                                               qk_prod[:, b % 2, g, :].rearrange("p (h d) -> p h d", d=HD), AX, ALU.add)
                    last.then_inc(prod_read, 1)

                v.wait_ge(params_in, l * 16 * N_PARAM_DMAS + 16 * N_PARAM_DMAS)
                tt(state[:, :, :], state[:, :, :], state_w.unsqueeze(1).to_broadcast([4 * BUF, 2, AW]), ALU.mult)\
                    .then_inc(st_ok, 1)
                glu(0)
                convolve(0)
                glu(1)
                glu(2)
                convolve(1, 0, 1)
                glu(3)
                convolve(1, 1)
                v.drain()
                v.wait_ge(st_ps, l + 1)
                for c in range(CH):
                    y = conv[:, c, SEQ:TOK]
                    v.tensor_scalar(y, u_smp[:, c, :], conv_w[:, c, BUF:TAPS], vec[:, CB + c:CB + c + 1],
                                    ALU.mult, ALU.add)
                    v.drain()
                    last = tt(y, y, bank[7][:, c * DEC:(c + 1) * DEC], ALU.add)
                last.then_inc(conv_ok, 1)
                rows_norm(0)
                v.tensor_copy(q_smp, qk_rows[0:DEC, 0, :]).then_inc(q_smp_ok, 1)
                tt(qk_new, qk_rows[0:DEC, 0, :], qk_rows[0:DEC, 1, :], ALU.mult)
                v.drain()
                v.tensor_reduce(sn[:, :], qk_new.rearrange("p (h d) -> p h d", d=HD), AX, ALU.add)
                v.drain()
                tt(sn_x[:, :].rearrange("p (b h) -> p b h", h=SUBS),
                   sn[:, :].unsqueeze(1).to_broadcast([DEC, DEC, SUBS]),
                   cs("own_seq", DEC).rearrange("p (b h) -> p b h", h=SUBS), ALU.mult)
                convolve(2)
                rows_norm(1)
                rows_norm(2)
                score_sums(0)
                score_sums(1)
                convolve(3)
                rows_norm(3)
                score_sums(2)
                score_sums(3)
                rows_norm(4)
                score_sums(4)
                score_sums(5)
                v.drain().then_inc(conv_ok, 1)

                def softmax_a(n):
                    qt, h = items[n]
                    width = (qt + 1) * P
                    v.wait_ge(s_ps, l * 16 + n + 1)
                    if n >= 2:
                        v.wait_ge(exp_ok, l * 16 + n - 1)
                    for j in range(2):
                        blk = bank[2 * (n % 2) + j][:, qt * P:width]
                        tt(blk, blk, cs("causal"), ALU.add)
                    v.drain()
                    for j in range(2):
                        v.tensor_reduce(mx[:, n % 2, 2 + j:3 + j], bank[2 * (n % 2) + j][:, 0:width], AX, ALU.max)
                    v.drain()
                    v.tensor_scalar(mx[:, n % 2, 0:2], mx[:, n % 2, 2:4], -SCALE, None, ALU.mult).then_inc(max_ok, 1)

                def softmax_b(n):
                    qt, h = items[n]
                    width = (qt + 1) * P
                    v.wait_ge(exp_ok, l * 16 + n + 1)
                    v.reciprocal(tmp[:, 0:2], zs[:, n % 2, :])
                    v.drain()
                    v.tensor_copy(rz[:, qt % 2, h:h + 1], tmp[:, 0:1])
                    v.tensor_scalar(tmp[:, 2:3], tmp[:, 1:2], zs[:, n % 2, 0:1], small[:, 4:5], ALU.mult, ALU.mult)
                    v.drain()
                    p0, p1 = probs[:, 2 * (n % 2), 0:width], probs[:, 2 * (n % 2) + 1, 0:width]
                    v.scalar_tensor_tensor(p0, p1, tmp[:, 2:3], p0, ALU.mult, ALU.add).then_inc(a_ok, 1)

                def finish_rows(qt):
                    o3 = o_rows.rearrange("p (h n) -> p h n", h=HEADS)
                    v.drain()
                    v.wait_ge(pv_ps, l * 16 + 4 * qt + 4)
                    if qt >= 1:
                        v.wait_ge(ot_ps, l * SAMPLE + qt)
                    tt(o3, bank[6][:, :].rearrange("p (h n) -> p h n", h=HEADS),
                       rz[:, qt % 2, :].unsqueeze(2).to_broadcast([P, HEADS, P]), ALU.mult).then_inc(o_ok, 1)
                    v.drain()
                    tt(o_sq, o_rows, o_rows, ALU.mult)
                    v.drain()
                    v.tensor_reduce(ss[:, 0:4], o_sq.rearrange("p (h n) -> p h n", h=HEADS), AX, ALU.add)
                    v.drain()
                    rsqrt(rs[:, 0:4], ss[:, 0:4], 4, 1.0 / VD)
                    tt(o3, o3, rs[:, 0:4].unsqueeze(2).to_broadcast([P, HEADS, P]), ALU.mult).then_inc(o_ok, 1)

                R = DEC * SUBS

                def centre():
                    v.wait_ge(mean_ps, l * 2 + 1)
                    v.scalar_tensor_tensor(conv[:, :, 0:SEQ], bank[7][:, :].unsqueeze(1).to_broadcast([P, CH, SEQ]),
                                           -1.0 / AW, conv[:, :, 0:SEQ], ALU.mult, ALU.add).then_inc(xc_ok, 1)

                def centre_sampled():
                    v.wait_ge(mean_ps, l * 2 + 2)
                    v.scalar_tensor_tensor(conv[:, :, SEQ:TOK],
                                           bank[7][:, 0:DEC].unsqueeze(1).to_broadcast([P, CH, DEC]),
                                           -1.0 / AW, conv[:, :, SEQ:TOK], ALU.mult, ALU.add).then_inc(xc_ok, 1)

                def sampled_max():
                    v.memset(wide_flat, 0.0)
                    v.wait_ge(dec_s, l + 1)
                    v.tensor_copy(s_dec[:, 0:PAST], bank[5][0:R, :])
                    v.tensor_copy(s_dec[:, PAST:PAST + 1], bank[7][0:R, 0:1])
                    v.drain()
                    v.tensor_reduce(small[0:R, 8:9], s_dec, AX, ALU.max)
                    v.drain()
                    v.tensor_scalar(small[0:R, 9:10], small[0:R, 8:9], -SCALE, None, ALU.mult).then_inc(dec_m, 1)

                def sampled_combine():
                    v.wait_ge(dec_e, l + 1)
                    v.reciprocal(small[0:R, 11:12], small[0:R, 10:11])
                    v.tensor_scalar(small[0:R, 12:13], cs("odd", R), small[0:R, 4:5], cs("even", R), ALU.mult, ALU.add)
                    v.drain()
                    tt(small[0:R, 13:14], small[0:R, 12:13], small[0:R, 11:12], ALU.mult)
                    v.tensor_scalar(c_dec[:, 32:40], cs("row_seq", R), s_dec[:, PAST:PAST + 1], None, ALU.mult)
                    v.drain()
                    v.tensor_scalar(c_dec[:, 0:32], cs("pair", R), small[0:R, 13:14], None, ALU.mult).then_inc(dec_c, 1)

                def sampled_weights_out():
                    v.wait_ge(dec_a, l + 1)
                    for b in range(DEC):
                        own = slice(b * HEADS, (b + 1) * HEADS)
                        v.tensor_copy(a_wide[:, b, :, own],
                                      bank[5][:, 0:P].rearrange("p (g n) -> p g n", g=PAGES)[:, :, own])
                    v.tensor_copy(a_new[:, :], bank[5][0:DEC, P:P + 32]).then_inc(dec_ok, 1)
                    v.memset(u_t[:, 3, 0:BUF], 0.0)

                v.wait_ge(ut_ps, l + 1)
                softmax_a(0)
                softmax_a(1)
                for n in range(16):
                    softmax_b(n)
                    if n + 2 < 16:
                        softmax_a(n + 2)
                    if n == 2:
                        score_sums(6)
                    if n == 3:
                        score_sums(7)
                        v.drain().then_inc(dec_in, 1)
                    if n == 6:
                        sampled_max()
                    if n == 7:
                        sampled_combine()
                    if n == 8:
                        sampled_weights_out()
                    if n == 12:
                        centre()
                    if n == 14:
                        centre_sampled()
                    if n % 4 == 0 and n >= 4:
                        finish_rows(n // 4 - 1)

                finish_rows(SAMPLE - 1)
                v.wait_ge(std_ok, l + 1)
                v.reciprocal(rs_conv, rs_conv)
                v.drain()
                tt(conv[:, :, :], conv[:, :, :], rs_conv.unsqueeze(1).to_broadcast([P, CH, TOK]), ALU.mult)\
                    .then_inc(cn_ok, 1)
                v.wait_ge(dec_t, l + 1)
                for h in range(HEADS):
                    v.tensor_copy(o_dec[:, 0, h * DEC:(h + 1) * DEC], bank[4][:, h * 32 + h:(h + 1) * 32:HEADS])
                v.drain()
                tt(o_dec[:, 1, :], o_dec[:, 0, :], o_dec[:, 0, :], ALU.mult).then_inc(dec_q, 1)
                v.wait_ge(dec_r, l + 1)
                rsqrt(o_dec[:, 2, :], bank[5][:, 0:32], 32, 1.0 / VD)
                tt(o_dec[:, 0, :], o_dec[:, 0, :], o_dec[:, 2, :], ALU.mult)
                v.drain()
                v.tensor_scalar(feat[:, 0:HEADS, SEQ:TOK], o_dec[:, 0, :].rearrange("p (h b) -> p h b", h=HEADS),
                                vec[:, SUB + 1:SUB + 2], None, ALU.mult).then_inc(dec_f, 1)

                v.wait_ge(x_again, l * 32 + 32)

                def turned(t):
                    n = rows_of[t]
                    for g in range(2):
                        v.wait_ge(turn2_ps, l * 10 + 2 * t + g + 1)
                        b = bank[4 + g][:, :].rearrange("p (c n) -> p c n", c=4)[:, :, 0:n]
                        tt(feat[:, 4 * g:4 * g + 4, cols(t)], b,
                           vec[:, G2 + 4 * g:G2 + 4 * g + 4].unsqueeze(2).to_broadcast([P, 4, n]), ALU.mult)\
                            .then_inc(feat2_ok, 1)

                for t in range(TILES):
                    n = rows_of[t]
                    v.wait_ge(wo_ps, l * TILES + t + 1)
                    for j in range(2):
                        xs = x[0:n, t, j * AW:(j + 1) * AW]
                        tt(xs, xs, bank[2 * (t % 2) + j][0:n, :], ALU.add)
                    v.drain().then_inc(x2_ok, 1)
                    v.wait_ge(sq2_ok, l * TILES + t + 1)
                    rsqrt(rs[0:n, t:t + 1], ss[0:n, t:t + 1], 1, 1.0 / D, n)
                    v.wait_ge(rows_out, l * 160 + 32 * t + 16)
                    v.tensor_scalar(x[0:n, t, :], x[0:n, t, :], rs[0:n, t:t + 1], None, ALU.mult).then_inc(xn2_ok, 1)
                    turned(t)
                    if t == 0:
                        v.memset(logit[:, SAMPLE, :], 0.0)
                        v.memset(chosen[:, TILES * EXPERTS:], 0.0)
                        for i in range(TILES):
                            for j, c in ((0, 0), (1, 1), (5, 2)):
                                at = where["tile_pay"][0] + i * 3 + c
                                v.tensor_copy(pay[:, i, :, j], const[:, at:at + 1].to_broadcast([P, EXPERTS]))

                v.wait_ge(log_ps, l * TILES + TILES)
                v.tensor_copy(logit[:, 0:SAMPLE, :], bank[6][:, 0:SAMPLE * 20].rearrange("p (t n) -> p t n", n=20))
                v.tensor_copy(logit[0:DEC, SAMPLE, :], bank[6][0:DEC, SAMPLE * 20:TILES * 20])
                v.drain()

                def grid(i, n=GROUPS):
                    return pick[:, i, 0:TILES * n].rearrange("p (t n) -> p t n", n=n)

                def over(i):
                    return few[:, i, :].unsqueeze(2).to_broadcast([P, TILES, GROUPS])

                index4 = cs("iota")[:, 0:GROUPS].unsqueeze(1).to_broadcast([P, TILES, GROUPS])

                def first_max(values, top, hit, scratch):
                    v.tensor_reduce(few[:, top, :], values, AX, ALU.max)
                    v.drain()
                    tt(scratch, values, over(top), ALU.is_equal)
                    v.drain()
                    v.scalar_tensor_tensor(scratch, scratch, -8.0, index4, ALU.mult, ALU.add)
                    v.drain()
                    v.tensor_reduce(few[:, 15, :], scratch, AX, ALU.min)
                    v.drain()
                    tt(hit, scratch, over(15), ALU.is_equal)
                    v.drain()

                lg = logit[:, :, 0:GROUPS]
                hit_g, hit1, hit2 = grid(3), pick[:, 4, 0:20].rearrange("p (t n) -> p t n", n=4), \
                    pick[:, 4, 20:40].rearrange("p (t n) -> p t n", n=4)
                scr = pick[:, 4, 40:60].rearrange("p (t n) -> p t n", n=4)
                el = pick[:, 3, 20:40].rearrange("p (t n) -> p t n", n=4)
                el2 = pick[:, 3, 40:60].rearrange("p (t n) -> p t n", n=4)
                first_max(lg, 0, hit_g, scr)
                tt(grid(1), lg, over(0), ALU.subtract)
                v.drain().then_inc(r_d, 1)
                wide = pick[:, 5, :].rearrange("p (t g j) -> p t g j", t=TILES, g=GROUPS)
                tt(wide, logit[:, :, GROUPS:].rearrange("p t (g j) -> p t g j", g=GROUPS),
                   hit_g.unsqueeze(3).to_broadcast([P, TILES, GROUPS, EPG]), ALU.mult)
                v.drain()
                v.tensor_reduce(el, pick[:, 5, :].rearrange("p (t g j) -> p t j g", t=TILES, g=GROUPS), AX, ALU.add)
                v.drain()
                first_max(el, 1, hit1, scr)
                v.scalar_tensor_tensor(el2, hit1, -BIG, el, ALU.mult, ALU.add)
                v.drain()
                first_max(el2, 2, hit2, scr)
                tt(few[:, 6, :], few[:, 2, :], few[:, 1, :], ALU.subtract)
                v.drain().then_inc(r_d, 1)
                v.wait_ge(r_e, l * 2 + 1)
                v.tensor_reduce(few[:, 3, :], grid(2), AX, ALU.add)
                v.wait_ge(r_e, l * 2 + 2)
                v.tensor_scalar(few[:, 8, :], few[:, 7, :], 1.0, None, ALU.add)
                v.drain()
                v.reciprocal(few[:, 4, :], few[:, 3, :])
                v.reciprocal(few[:, 9, :], few[:, 8, :])
                for i, hit in ((1, hit1), (2, hit2)):
                    tt(pick[:, i, :].rearrange("p (t g j) -> p t g j", t=TILES, g=GROUPS),
                       hit_g.unsqueeze(3).to_broadcast([P, TILES, GROUPS, EPG]),
                       hit.unsqueeze(2).to_broadcast([P, TILES, GROUPS, EPG]), ALU.mult)
                v.drain()
                tt(few[:, 10, :], few[:, 9, :], few[:, 4, :], ALU.mult)
                t16 = [pick[:, i, :].rearrange("p (t e) -> p t e", t=TILES) for i in range(6)]
                t16[0] = chosen[:, 0:TILES * EXPERTS].rearrange("p (t e) -> p t e", t=TILES)
                tt(t16[0], t16[1], t16[2], ALU.add)
                v.drain()
                tt(few[:, 11, :], few[:, 10, :], few[:, 7, :], ALU.mult)
                tt(t16[0], t16[0], cs("valid").unsqueeze(2).to_broadcast([P, TILES, EXPERTS]), ALU.mult)
                v.drain().then_inc(m_ok, 1)
                for i in (1, 2):
                    tt(t16[i], t16[i], few[:, 9 + i, :].unsqueeze(2).to_broadcast([P, TILES, EXPERTS]), ALU.mult)
                v.drain()
                tt(t16[3], t16[1], t16[2], ALU.add)
                v.drain()
                v.tensor_copy(pay[:, :, :, 2], t16[3])
                v.drain()
                tt(t16[4], t16[3], pay[:, :, :, 2], ALU.subtract)
                v.drain()
                v.tensor_copy(pay[:, :, :, 3], t16[4])
                v.drain()
                tt(pay[:, :, :, 4], t16[4], pay[:, :, :, 3], ALU.subtract)
                v.wait_ge(cum_ps, l + 1)
                v.scalar_tensor_tensor(key[:, :, :], bank[7][:, 0:80].rearrange("p (t e) -> p t e", t=TILES), 1.0,
                                       t16[0], ALU.add, ALU.mult)
                v.tensor_copy(cnt[:, :], bank[7][:, 80:96])
                v.drain()
                v.tensor_scalar(key[:, :, :], key[:, :, :], -1.0, None, ALU.add)
                v.drain()
                iota = cs("iota").unsqueeze(1).to_broadcast([P, TILES, P])

                def slot_rows(src, row, g, f):
                    v.tensor_copy(f[:, :, 3:], src)
                    v.drain()
                    src = f[:, :, 3:]
                    v.scalar_tensor_tensor(f[:, :, 0], src[:, :, 1], float(P), src[:, :, 0], ALU.mult, ALU.add)
                    v.tensor_scalar(f[:, :, 1], src[:, :, 5], -1.0, 1.0, ALU.mult, ALU.add)
                    v.tensor_copy(f[:, :, 2], src[:, :, 2])
                    v.drain()
                    tt(g, f[:, :, 2], src[:, :, 3], ALU.add)
                    v.scalar_tensor_tensor(f[:, :, 0], f[:, :, 1], cs("pad_row"), f[:, :, 0], ALU.mult, ALU.add)
                    v.drain()
                    v.tensor_copy(row, f[:, :, 0])
                    return tt(g, g, src[:, :, 4], ALU.add)

                for e in range(EXPERTS):
                    if e >= 2:
                        v.wait_ge(idx_ps, l * EXPERTS + e - 1)
                    tt(hot[:, e % 2, :, :], iota, key[:, :, e:e + 1].to_broadcast([P, TILES, P]), ALU.is_equal)\
                        .then_inc(hot_ok, 1)
                v.wait_ge(idx_ps, l * EXPERTS + EXPERTS)
                slot_rows(bank[0][:, 0:EXPERTS * PAY].rearrange("p (e c) -> p e c", c=PAY), rows_g[:, 0:EXPERTS],
                          gate[:, 0:EXPERTS], slot_f[:, :, :])
                v.drain().then_inc(idx_ok, 1)
                def rows_turned(b, g, src):
                    return tt(xe_t[:, b, 4 * g:4 * g + 4, :], src[:, :].rearrange("p (c n) -> p c n", c=4),
                              vec[:, G2 + 4 * g:G2 + 4 * g + 4].unsqueeze(2).to_broadcast([P, 4, P]), ALU.mult)

                def features(b, n):
                    for g in range(2):
                        v.wait_ge(xt_ps, n * 2 + (g + 1))
                        rows_turned(b, g, bank[6 + g]).then_inc(xt_ok, 1)

                def hidden(b, n):
                    v.wait_ge(silu_ok, n + 1)
                    tt(hid[:, b, :], hid[:, b, :], bank[3 + 2 * b][:, :], ALU.mult).then_inc(hid_ok, 1)

                def y_half(b, n, e):
                    v.wait_ge(dn_ps, n + 1)
                    v.wait_ge(y_add, n * 16 + 16)
                    v.tensor_scalar(ye[:, b, F:], bank[1][:, :], gate[:, bass.ds(e, 1)], None, ALU.mult)\
                        .then_inc(y_ok, 1)

                features(0, v.snap(l * EXPERTS))
                features(1, v.snap(l * EXPERTS + 1))
                S = MAX_SPILL
                n_pairs = EXPERTS * SPILL_J
                flag, run = pick[:, 1, 0:n_pairs], pick[:, 2, 0:n_pairs]
                tt(flag.rearrange("p (e j) -> p e j", j=SPILL_J),
                   cnt[:, :].unsqueeze(2).to_broadcast([P, EXPERTS, SPILL_J]),
                   cs("spill_j").rearrange("p (e j) -> p e j", j=SPILL_J), ALU.is_gt)
                v.drain()
                v.tensor_tensor_scan(out=run, data0=ones[:, 0:n_pairs], data1=flag, initial=0.0,
                                     op0=ALU.mult, op1=ALU.add)
                v.tensor_copy(sp_f[:, 1:2], sp_f[:, 18:19])
                v.drain()
                v.tensor_copy(sp_f[:, 0:1], run[:, n_pairs - 1:n_pairs])
                tt(spill_a, run.unsqueeze(1).to_broadcast([P, S, n_pairs]),
                   cs("spill_no").unsqueeze(2).to_broadcast([P, S, n_pairs]), ALU.is_equal)
                v.drain()
                tt(sp_f[:, 18:19], sp_f[:, 1:2], sp_f[:, 0:1], ALU.add)
                tt(spill_a, spill_a, flag.unsqueeze(1).to_broadcast([P, S, n_pairs]), ALU.mult)
                v.drain()
                for name, at in (("expert_of", 2), ("spill_j", 10)):
                    tt(spill_b, spill_a, cs(name).unsqueeze(1).to_broadcast([P, S, n_pairs]), ALU.mult)
                    v.drain()
                    v.tensor_reduce(sp_f[:, at:at + S], spill_b, AX, ALU.add)
                    v.drain()
                v.tensor_copy(sp_i[0:1, 0:2 + S], sp_f[0:1, 0:2 + S])
                v.drain().then_inc(spill_ok, 1)

                with v.Fori(0, EXPERTS // 2 - 1) as g:
                    n = v.snap(l * EXPERTS + g * 2)
                    hidden(0, n)
                    features(0, n + 2)
                    y_half(0, n, g * 2)
                    hidden(1, n + 1)
                    features(1, n + 3)
                    y_half(1, n + 1, g * 2 + 1)
                n = v.snap(l * EXPERTS + EXPERTS - 2)
                hidden(0, n)
                y_half(0, n, EXPERTS - 2)
                hidden(1, n + 1)
                y_half(1, n + 1, EXPERTS - 1)
                n_spill = v.value_load(sp_i[0:1, 0:1], min_val=0, max_val=MAX_SPILL)
                before = v.value_load(sp_i[0:1, 1:2], min_val=0, max_val=DEPTH * MAX_SPILL)
                with v.If(n_spill > 0):
                    with v.Fori(0, n_spill) as i:
                        m = v.snap(before + i)
                        e = v.value_load(sp_i[0:1, bass.ds(i + 2, 1)], min_val=0, max_val=EXPERTS - 1)
                        v.tensor_scalar(few[:, 12, :].unsqueeze(2), key[:, :, bass.ds(e, 1)],
                                        sp_f[:, bass.ds(i + 10, 1)], None, ALU.subtract)
                        v.drain()
                        tt(hot[:, 0, :, :], iota, few[:, 12, :].unsqueeze(2).to_broadcast([P, TILES, P]), ALU.is_equal)\
                            .then_inc(sp_hot, 1)
                        v.wait_ge(sp_idx, m + 1)
                        slot_rows(bank[0][:, 0:PAY].unsqueeze(1), rows_g[:, EXPERTS:EXPERTS + 1],
                                  gate[:, EXPERTS:EXPERTS + 1], slot_f[:, 0:1, :])
                        v.drain().then_inc(sp_rows, 1)
                        v.wait_ge(sp_xt, m + 1)
                        rows_turned(0, 0, bank[6])
                        rows_turned(0, 1, bank[7]).then_inc(sp_xtok, 1)
                        v.wait_ge(sp_silu, m + 1)
                        tt(hid[:, 0, :], hid[:, 0, :], bank[3][:, :], ALU.mult).then_inc(sp_hid, 1)
                        v.wait_ge(sp_dn, m + 1)
                        v.tensor_scalar(ye[:, 0, F:], bank[1][:, :], gate[:, EXPERTS:EXPERTS + 1], None, ALU.mult)\
                            .then_inc(sp_y, 1)
                        v.wait_ge(sp_add, m * 16 + 16)


_INS = ["x_prompt", "x_sample", "cache_k", "cache_v", "state_conv", "page_table", "w_in", "conv_w", "w_out",
        "w_gate", "w_up", "w_down"]
_VECTORS = ["norm1_g", "norm2_g", "conv_b", "conv_ln_g", "conv_ln_b", "subln_g"]
_HEADS = ["q_norm_g", "k_norm_g", "lam_q1", "lam_k1", "lam_q2", "lam_k2"]
_ROUTERS = ["w_router_group", "w_router_expert"]
_OUTS = [("y_prompt", (1, SEQ, D)), ("y_sample", (DEC, 1, D)), ("k_prompt", (DEPTH, 1, SEQ, SUBS, HD)),
         ("v_prompt", (DEPTH, 1, SEQ, HEADS, VD)), ("conv_prompt", (DEPTH, 1, BUF, AW)),
         ("k_sample", (DEPTH, DEC, 1, SUBS, HD)), ("v_sample", (DEPTH, DEC, 1, HEADS, VD)),
         ("conv_sample", (DEPTH, DEC, BUF, AW))]


def kernel(**inputs):
    import concourse.bacc as _bacc
    from concourse.bass_utils import run_bass_kernel_spmd as _run

    nc = _bacc.Bacc("TRN2", target_bir_lowering=False, num_devices=1)
    arrays, aps = {}, {}

    def give(name, value):
        arrays[f"in_{name}"] = value
        aps[name] = nc.dram_tensor(f"in_{name}", value.shape, mybir.dt.from_np(value.dtype), kind="ExternalInput").ap()

    for name in _INS:
        give(name, np.ascontiguousarray(inputs[name]))
    vectors = [np.asarray(inputs[name]).reshape(DEPTH, -1, P) for name in _VECTORS]
    give("vectors", np.ascontiguousarray(np.concatenate(vectors, axis=1)))
    give("heads", np.ascontiguousarray(np.concatenate([np.asarray(inputs[name]) for name in _HEADS], axis=1)))
    give("w_router", np.ascontiguousarray(np.concatenate([np.asarray(inputs[name]) for name in _ROUTERS], axis=2)))
    give("const", const_table())
    first = [0.8 - 0.6 * math.exp(-0.3 * i) for i in range(DEPTH)]
    give("lam_init", np.array([[z, 1.0 - z] for z in first], np.float32))
    outs = {name: nc.dram_tensor(f"out_{name}", shape, F32, kind="ExternalOutput").ap() for name, shape in _OUTS}
    x_rows = nc.dram_tensor("x_rows", (TOK + P, D), F32, kind="Internal").ap()
    xn_rows = nc.dram_tensor("xn_rows", (TOK, D), F32, kind="Internal").ap()
    hybrid_step(nc, aps, outs, x_rows, xn_rows)
    r = _run(nc, [arrays], core_ids=[0])
    return tuple(r.results[0][f"out_{name}"] for name, _ in _OUTS)
```
